# Optimizing a Trainium2 kernel written in Bass

```python
import jax, jax.numpy as jnp
from jax import lax
import numpy as np
import math

D_MODEL = 1024
BATCH = 1
SEQ = 256
DEPTH = 2

GRID_W = 64
CTX_LEN = 256
N_MIXERS = 2
N_A = (DEPTH + 1) // 2
N_B = DEPTH // 2
MLA_HEADS = 8
QK_NOPE = 128
QK_ROPE = 64
V_DIM = 128
QK_DIM = QK_NOPE + QK_ROPE
Q_LORA = 384
KV_LORA = 256
ROPE_THETA = 10000.0
Q_BLOCK = 128
GM_CHUNK = 128
GM_GROUPS = 8
GM_HALF = 2 * D_MODEL
GM_GROUP_DIM = GM_HALF // GM_GROUPS
FFN_HIDDEN = 4 * D_MODEL
N_MOD = 6
EPS = 1e-6


def rmsnorm(x, g):
    xf = x.astype(jnp.float32)
    y = xf * lax.rsqrt(jnp.mean(xf * xf, axis=-1, keepdims=True) + EPS)
    return (y * g.astype(jnp.float32)).astype(x.dtype)

def layernorm(x, g, b):
    xf = x.astype(jnp.float32)
    mu = jnp.mean(xf, axis=-1, keepdims=True)
    var = jnp.mean(jnp.square(xf - mu), axis=-1, keepdims=True)
    y = (xf - mu) * lax.rsqrt(var + EPS)
    return (y * g.astype(jnp.float32) + b.astype(jnp.float32)).astype(x.dtype)

def modulate(x, g, shift, scale):
    return rmsnorm(x, g) * (1.0 + scale) + shift

def axial_rope_tables(n_tokens, dtype):
    rows = n_tokens // GRID_W
    row = jnp.repeat(jnp.arange(rows, dtype=jnp.float32), GRID_W)
    col = jnp.tile(jnp.arange(GRID_W, dtype=jnp.float32), rows)
    half = QK_ROPE // 2
    inv = ROPE_THETA ** (-jnp.arange(0, half, 2, dtype=jnp.float32) / half)
    ang_r = row[:, None] * inv[None, :]
    ang_c = col[:, None] * inv[None, :]
    ang = jnp.concatenate([ang_r, ang_r, ang_c, ang_c], axis=-1)
    return jnp.cos(ang).astype(dtype), jnp.sin(ang).astype(dtype)

def rotate_axial(x):
    a1, a2, b1, b2 = jnp.split(x, 4, axis=-1)
    return jnp.concatenate([-a2, a1, -b2, b1], axis=-1)

def rope_part(t, cos, sin):
    nope, pe = t[..., :QK_NOPE], t[..., QK_NOPE:]
    c = cos[None, :, None, :]
    s = sin[None, :, None, :]
    return jnp.concatenate([nope, pe * c + rotate_axial(pe) * s], axis=-1)

def block_attention(q, k, v, scale):
    B, Sq, H, Dk = q.shape
    nb = Sq // Q_BLOCK
    qb = q.reshape(B, nb, Q_BLOCK, H, Dk).transpose(1, 0, 2, 3, 4)

    def one(qi):
        s = jnp.einsum('bqhd,bkhd->bhqk', qi, k, preferred_element_type=jnp.float32) * scale
        p = jax.nn.softmax(s, axis=-1)
        return jnp.einsum('bhqk,bkhd->bqhd', p.astype(v.dtype), v)

    o = lax.map(one, qb)
    return o.transpose(1, 0, 2, 3, 4).reshape(B, Sq, H, v.shape[-1])

def mla_queries(h, wq_a, q_a_norm, wq_b, q_norm):
    B, S, _ = h.shape
    cq = rmsnorm(h @ wq_a, q_a_norm)
    q = (cq @ wq_b).reshape(B, S, MLA_HEADS, QK_DIM)
    return rmsnorm(q, q_norm)

def mla_keys_values(h, wkv_a, kv_a_norm, wkv_b, k_norm):
    B, S, _ = h.shape
    kv_a = h @ wkv_a
    ckv, k_pe = kv_a[..., :KV_LORA], kv_a[..., KV_LORA:]
    kv = (rmsnorm(ckv, kv_a_norm) @ wkv_b).reshape(B, S, MLA_HEADS, QK_NOPE + V_DIM)
    k_nope, v = kv[..., :QK_NOPE], kv[..., QK_NOPE:]
    k_pe = jnp.broadcast_to(k_pe[:, :, None, :], (B, S, MLA_HEADS, QK_ROPE))
    k = rmsnorm(jnp.concatenate([k_nope, k_pe], axis=-1), k_norm)
    return k, v

def mla_mixer(h_lat, h_ctx, cos, sin, wq_a, q_a_norm, wq_b, wkv_a, kv_a_norm, wkv_b,
              q_norm, k_norm, wo, with_ctx):
    B, S, _ = h_lat.shape
    scale = QK_DIM ** -0.5
    k_lat, v_lat = mla_keys_values(h_lat, wkv_a, kv_a_norm, wkv_b, k_norm)
    k_ctx, v_ctx = mla_keys_values(h_ctx, wkv_a, kv_a_norm, wkv_b, k_norm)
    k_lat = rope_part(k_lat, cos, sin)
    q_lat = rope_part(mla_queries(h_lat, wq_a, q_a_norm, wq_b, q_norm), cos, sin)
    k_all = jnp.concatenate([k_ctx, k_lat], axis=1)
    v_all = jnp.concatenate([v_ctx, v_lat], axis=1)
    o_lat = block_attention(q_lat, k_all, v_all, scale).reshape(B, S, MLA_HEADS * V_DIM) @ wo
    o_ctx = None
    if with_ctx:
        q_ctx = mla_queries(h_ctx, wq_a, q_a_norm, wq_b, q_norm)
        o_ctx = block_attention(q_ctx, k_ctx, v_ctx, scale).reshape(
            B, h_ctx.shape[1], MLA_HEADS * V_DIM) @ wo
    return o_lat, o_ctx

def gmlp_mixer(h, w_in, ln_g, ln_b, ws, bs, w_out):
    B, S, _ = h.shape
    z = jax.nn.gelu(h @ w_in, approximate=False)
    u, v = z[..., :GM_HALF], z[..., GM_HALF:]
    v = layernorm(v, ln_g, ln_b)
    vc = v.reshape(B, S // GM_CHUNK, GM_CHUNK, GM_GROUPS, GM_GROUP_DIM)
    mixed = jnp.einsum('gpq,bnqgc->bnpgc', ws, vc) + bs.T[None, None, :, :, None]
    return (u * mixed.reshape(B, S, GM_HALF)) @ w_out

def squared_relu_mlp(h, w1, w2):
    return jnp.square(jax.nn.relu(h @ w1)) @ w2

def first_inputs(seed: int = 0) -> dict:
    key = jax.random.key(seed)
    ks = jax.random.split(key, 32)
    D = D_MODEL

    def nrm(k, shape, scale):
        return jax.random.normal(k, shape, jnp.float32) * scale

    def gain(k, shape):
        return 1.0 + 0.05 * jax.random.normal(k, shape, jnp.float32)

    return {
        "x": nrm(ks[0], (BATCH, SEQ, D), 1.0),
        "c": nrm(ks[1], (BATCH, D), 1.0),
        "ctx": nrm(ks[2], (BATCH, CTX_LEN, D), 1.0),
        "c_ctx": nrm(ks[3], (D,), 1.0),
        "ada_w": nrm(ks[4], (DEPTH, D, N_MOD * D), 0.5 * D ** -0.5),
        "ada_b": nrm(ks[5], (DEPTH, N_MOD * D), 0.01),
        "norm_mix_g": gain(ks[6], (DEPTH, D)),
        "norm_ffn_g": gain(ks[7], (DEPTH, D)),
        "mla_wq_a": nrm(ks[8], (N_A, D, Q_LORA), D ** -0.5),
        "mla_q_a_norm": gain(ks[9], (N_A, Q_LORA)),
        "mla_wq_b": nrm(ks[10], (N_A, Q_LORA, MLA_HEADS * QK_DIM), Q_LORA ** -0.5),
        "mla_wkv_a": nrm(ks[11], (N_A, D, KV_LORA + QK_ROPE), D ** -0.5),
        "mla_kv_a_norm": gain(ks[12], (N_A, KV_LORA)),
        "mla_wkv_b": nrm(ks[13], (N_A, KV_LORA, MLA_HEADS * (QK_NOPE + V_DIM)), KV_LORA ** -0.5),
        "mla_q_norm": gain(ks[14], (N_A, QK_DIM)),
        "mla_k_norm": gain(ks[15], (N_A, QK_DIM)),
        "mla_wo": nrm(ks[16], (N_A, MLA_HEADS * V_DIM, D), (MLA_HEADS * V_DIM) ** -0.5),
        "gm_w_in": nrm(ks[17], (N_B, D, 2 * GM_HALF), D ** -0.5),
        "gm_ln_g": gain(ks[18], (N_B, GM_HALF)),
        "gm_ln_b": nrm(ks[19], (N_B, GM_HALF), 0.02),
        "gm_ws": nrm(ks[20], (N_B, GM_GROUPS, GM_CHUNK, GM_CHUNK), GM_CHUNK ** -0.5),
        "gm_bs": gain(ks[21], (N_B, GM_GROUPS, GM_CHUNK)),
        "gm_w_out": nrm(ks[22], (N_B, GM_HALF, D), GM_HALF ** -0.5),
        "ffn_w1": nrm(ks[23], (DEPTH, D, FFN_HIDDEN), D ** -0.5),
        "ffn_w2": nrm(ks[24], (DEPTH, FFN_HIDDEN, D), FFN_HIDDEN ** -0.5),
    }

def first_block(x, c, ctx, c_ctx, ada_w, ada_b, norm_mix_g, norm_ffn_g,
              mla_wq_a, mla_q_a_norm, mla_wq_b, mla_wkv_a, mla_kv_a_norm, mla_wkv_b,
              mla_q_norm, mla_k_norm, mla_wo,
              gm_w_in, gm_ln_g, gm_ln_b, gm_ws, gm_bs, gm_w_out,
              ffn_w1, ffn_w2):
    S = x.shape[1]
    cos, sin = axial_rope_tables(S, x.dtype)
    silu_c = jax.nn.silu(c)
    silu_cc = jax.nn.silu(c_ctx)
    y = ctx
    for i in range(DEPTH):
        with_ctx = i < DEPTH - 1
        use_mla = (i % N_MIXERS) == 0
        j = i // N_MIXERS
        m_lat = (silu_c @ ada_w[i] + ada_b[i])[:, None, :]
        m_ctx = silu_cc @ ada_w[i] + ada_b[i]
        sh_m, sc_m, g_m, sh_f, sc_f, g_f = jnp.split(m_lat, N_MOD, axis=-1)
        csh_m, csc_m, cg_m, csh_f, csc_f, cg_f = jnp.split(m_ctx, N_MOD, axis=-1)

        h_lat = modulate(x, norm_mix_g[i], sh_m, sc_m)
        if use_mla:
            h_ctx = modulate(y, norm_mix_g[i], csh_m, csc_m)
            o_lat, o_ctx = mla_mixer(h_lat, h_ctx, cos, sin, mla_wq_a[j], mla_q_a_norm[j],
                                     mla_wq_b[j], mla_wkv_a[j], mla_kv_a_norm[j], mla_wkv_b[j],
                                     mla_q_norm[j], mla_k_norm[j], mla_wo[j], with_ctx)
        else:
            o_lat = gmlp_mixer(h_lat, gm_w_in[j], gm_ln_g[j], gm_ln_b[j], gm_ws[j], gm_bs[j],
                               gm_w_out[j])
            o_ctx = None
            if with_ctx:
                h_ctx = modulate(y, norm_mix_g[i], csh_m, csc_m)
                o_ctx = gmlp_mixer(h_ctx, gm_w_in[j], gm_ln_g[j], gm_ln_b[j], gm_ws[j], gm_bs[j],
                                   gm_w_out[j])
        x = x + g_m * o_lat
        x = x + g_f * squared_relu_mlp(modulate(x, norm_ffn_g[i], sh_f, sc_f), ffn_w1[i], ffn_w2[i])
        if with_ctx:
            y = y + cg_m * o_ctx
            y = y + cg_f * squared_relu_mlp(modulate(y, norm_ffn_g[i], csh_f, csc_f),
                                            ffn_w1[i], ffn_w2[i])
    return x


REL_BUCKETS = 32
REL_MAX_EXACT = 16
REL_MAX_DIST = 128
ATTN_HEADS = 8

GLA_HEADS = 4
GLA_DK = 64
GLA_DV = 128
GLA_RANK = 16
GLA_TAU = 16.0
GLA_CHUNK = 64

SWA_HEADS = ATTN_HEADS
SWA_KV_HEADS = 2
SWA_DH = 64
SWA_WINDOW = 128

MOBA_HEADS = ATTN_HEADS
MOBA_KV_HEADS = 2
MOBA_DH = 128
MOBA_BLOCK = 256
MOBA_TOPK = 3
MOBA_Q_CHUNK = 32


A_WIDTH = GLA_HEADS * GLA_DV
B_WIDTH = SWA_HEADS * SWA_DH
C_WIDTH = MOBA_HEADS * MOBA_DH
EVEN_WIDTH = A_WIDTH + B_WIDTH
EVEN_SPLITS = (GLA_HEADS * GLA_DK, GLA_HEADS * GLA_DK, A_WIDTH, GLA_RANK, A_WIDTH,
               B_WIDTH, SWA_KV_HEADS * SWA_DH, SWA_KV_HEADS * SWA_DH, B_WIDTH)
EVEN_COLS = 2832
ODD_SPLITS = (C_WIDTH, MOBA_KV_HEADS * MOBA_DH, MOBA_KV_HEADS * MOBA_DH, C_WIDTH)
ODD_COLS = 2560
N_EVEN = (DEPTH + 1) // 2
N_ODD = DEPTH // 2


def rmsnorm_2(x, g):
    xf = x.astype(jnp.float32)
    y = xf * lax.rsqrt(jnp.mean(xf * xf, axis=-1, keepdims=True) + EPS)
    return (y * g.astype(jnp.float32)).astype(x.dtype)

def split_cols(h, sizes):
    idx = np.cumsum(np.array(sizes))[:-1].tolist()
    return jnp.split(h, idx, axis=-1)

def t5_bucket(dist):
    n = jnp.maximum(dist, 0)
    nf = jnp.maximum(n, 1).astype(jnp.float32)
    large = REL_MAX_EXACT + (jnp.log(nf / REL_MAX_EXACT) / math.log(REL_MAX_DIST / REL_MAX_EXACT)
                             * (REL_BUCKETS - REL_MAX_EXACT)).astype(jnp.int32)
    large = jnp.minimum(large, REL_BUCKETS - 1)
    return jnp.where(n < REL_MAX_EXACT, n, large)

def gla_chunked(q, k, v, log_a):
    B_, S_, H_, DK = q.shape
    DV = v.shape[-1]
    N = S_ // GLA_CHUNK

    def chunks(t):
        return t.astype(jnp.float32).reshape(B_, N, GLA_CHUNK, H_, t.shape[-1]).transpose(0, 3, 1, 2, 4)

    qc, kc, vc, gc = chunks(q), chunks(k), chunks(v), chunks(log_a)
    b = jnp.cumsum(gc, axis=3)
    b_last = b[:, :, :, -1:, :]
    q_e = qc * jnp.exp(b) * (DK ** -0.5)
    k_e = kc * jnp.exp(-b)
    causal = jnp.tril(jnp.ones((GLA_CHUNK, GLA_CHUNK), dtype=bool))
    att = jnp.where(causal, jnp.einsum('bhncd,bhnsd->bhncs', q_e, k_e), 0.0)
    o_intra = jnp.einsum('bhncs,bhnse->bhnce', att, vc)
    kv_chunk = jnp.einsum('bhncd,bhnce->bhnde', kc * jnp.exp(b_last - b), vc)
    decay = jnp.exp(b_last[:, :, :, 0, :])

    def step(state, inp):
        dec, kv = inp
        return dec[..., None] * state + kv, state

    s0 = jnp.zeros((B_, H_, DK, DV), jnp.float32)
    _, s_before = lax.scan(step, s0, (jnp.moveaxis(decay, 2, 0), jnp.moveaxis(kv_chunk, 2, 0)))
    s_before = jnp.moveaxis(s_before, 0, 2)
    o = o_intra + jnp.einsum('bhncd,bhnde->bhnce', q_e, s_before)
    return o.transpose(0, 2, 3, 1, 4).reshape(B_, S_, H_, DV).astype(v.dtype)

def swa_attention(q, k, v, sinks, rel_bias):
    B_, S_, H_, DH = q.shape
    KVH = k.shape[2]
    G = H_ // KVH
    W = SWA_WINDOW
    NB = S_ // W
    qb = q.reshape(B_, NB, W, KVH, G, DH).transpose(0, 3, 4, 1, 2, 5)

    def band(t):
        tb = t.reshape(B_, NB, W, KVH, DH).transpose(0, 3, 1, 2, 4)
        prev = jnp.pad(tb[:, :, :-1], ((0, 0), (0, 0), (1, 0), (0, 0), (0, 0)))
        return jnp.concatenate([prev, tb], axis=3)

    kb, vb = band(k), band(v)
    qi = jnp.arange(W)[:, None]
    kj = jnp.arange(2 * W)[None, :]
    dist = qi + W - kj
    in_win = (dist >= 0) & (dist < W)
    blk = jnp.arange(NB)[:, None, None]
    mask = in_win[None] & ((blk > 0) | (kj[None] >= W))
    bias = rel_bias[t5_bucket(dist)].astype(jnp.float32)
    bias = bias.transpose(2, 0, 1).reshape(KVH, G, 1, W, 2 * W)
    logits = jnp.einsum('bkgnqd,bknsd->bkgnqs', qb, kb).astype(jnp.float32) * (DH ** -0.5) + bias
    logits = jnp.where(mask, logits, -jnp.inf)
    sink = jnp.broadcast_to(sinks.astype(jnp.float32).reshape(KVH, G, 1, 1, 1), logits.shape[:-1] + (1,))
    probs = jax.nn.softmax(jnp.concatenate([logits, sink], axis=-1), axis=-1)[..., :-1]
    o = jnp.einsum('bkgnqs,bknsd->bkgnqd', probs.astype(v.dtype), vb)
    return o.transpose(0, 3, 4, 1, 2, 5).reshape(B_, S_, H_ * DH)

def moba_attention(q, k, v, rel_bias):
    B_, S_, H_, DH = q.shape
    G = H_ // k.shape[2]
    S_pad = -(-S_ // MOBA_BLOCK) * MOBA_BLOCK
    pad = ((0, 0), (0, S_pad - S_), (0, 0), (0, 0))
    qh = jnp.pad(q, pad).transpose(0, 2, 1, 3)
    kh = jnp.repeat(jnp.pad(k, pad), G, axis=2).transpose(0, 2, 1, 3)
    vh = jnp.repeat(jnp.pad(v, pad), G, axis=2).transpose(0, 2, 1, 3)
    NBLK = S_pad // MOBA_BLOCK
    kblk = kh.reshape(B_, H_, NBLK, MOBA_BLOCK, DH)
    vblk = vh.reshape(B_, H_, NBLK, MOBA_BLOCK, DH)
    kmean = kblk.mean(axis=3)
    k_sel = min(MOBA_TOPK, NBLK)
    bi = jnp.arange(B_)[:, None, None, None]
    hi = jnp.arange(H_)[None, :, None, None]
    offs = jnp.arange(MOBA_BLOCK)
    blk_ids = jnp.arange(NBLK)
    scale = DH ** -0.5

    def one_chunk(c):
        start = c * MOBA_Q_CHUNK
        qc = lax.dynamic_slice_in_dim(qh, start, MOBA_Q_CHUNK, axis=2)
        tpos = start + jnp.arange(MOBA_Q_CHUNK)
        own = start // MOBA_BLOCK
        gate = jnp.einsum('bhqd,bhnd->bhqn', qc, kmean).astype(jnp.float32)
        gate = jnp.where(blk_ids < own, gate, -jnp.inf)
        _, idx = lax.top_k(gate, k_sel)
        kg = kblk[bi, hi, idx].reshape(B_, H_, MOBA_Q_CHUNK, k_sel * MOBA_BLOCK, DH)
        vg = vblk[bi, hi, idx].reshape(B_, H_, MOBA_Q_CHUNK, k_sel * MOBA_BLOCK, DH)
        kpos = (idx[..., None] * MOBA_BLOCK + offs).reshape(B_, H_, MOBA_Q_CHUNK, k_sel * MOBA_BLOCK)
        valid = jnp.broadcast_to((idx < own)[..., None], idx.shape + (MOBA_BLOCK,)).reshape(kpos.shape)
        bias_sel = rel_bias[t5_bucket(tpos[None, None, :, None] - kpos), hi].astype(jnp.float32)
        logit_sel = jnp.einsum('bhqd,bhqsd->bhqs', qc, kg).astype(jnp.float32) * scale + bias_sel
        logit_sel = jnp.where(valid, logit_sel, -jnp.inf)
        ko = lax.dynamic_slice_in_dim(kh, own * MOBA_BLOCK, MOBA_BLOCK, axis=2)
        vo = lax.dynamic_slice_in_dim(vh, own * MOBA_BLOCK, MOBA_BLOCK, axis=2)
        dist_own = tpos[:, None] - (own * MOBA_BLOCK + offs)[None, :]
        bias_own = rel_bias[t5_bucket(dist_own)].astype(jnp.float32).transpose(2, 0, 1)
        logit_own = jnp.einsum('bhqd,bhsd->bhqs', qc, ko).astype(jnp.float32) * scale + bias_own
        logit_own = jnp.where(dist_own >= 0, logit_own, -jnp.inf)
        probs = jax.nn.softmax(jnp.concatenate([logit_sel, logit_own], axis=-1), axis=-1)
        p_sel = probs[..., :k_sel * MOBA_BLOCK]
        p_own = probs[..., k_sel * MOBA_BLOCK:]
        o = jnp.einsum('bhqs,bhqsd->bhqd', p_sel, vg) + jnp.einsum('bhqs,bhsd->bhqd', p_own, vo)
        return o.astype(v.dtype)

    out = lax.map(one_chunk, jnp.arange(S_pad // MOBA_Q_CHUNK))
    out = out.transpose(1, 0, 3, 2, 4).reshape(B_, S_pad, H_ * DH)
    return out[:, :S_]

def even_layer(hn, w_in, gla_w_up, gla_b_up, gla_gain, sinks, w_out, rel_bias):
    B_, S_, _ = hn.shape
    proj = hn @ w_in
    aq, ak, av, a_down, a_gate, bq, bk, bv, b_gate = split_cols(proj, EVEN_SPLITS)
    log_a = jax.nn.log_sigmoid((a_down @ gla_w_up + gla_b_up).astype(jnp.float32)) / GLA_TAU
    oa = gla_chunked(aq.reshape(B_, S_, GLA_HEADS, GLA_DK), ak.reshape(B_, S_, GLA_HEADS, GLA_DK),
                     av.reshape(B_, S_, GLA_HEADS, GLA_DV), log_a.reshape(B_, S_, GLA_HEADS, GLA_DK))
    oa = rmsnorm_2(oa, gla_gain).reshape(B_, S_, A_WIDTH) * jax.nn.silu(a_gate)
    ob = swa_attention(bq.reshape(B_, S_, SWA_HEADS, SWA_DH), bk.reshape(B_, S_, SWA_KV_HEADS, SWA_DH),
                       bv.reshape(B_, S_, SWA_KV_HEADS, SWA_DH), sinks, rel_bias) * jax.nn.silu(b_gate)
    return jnp.concatenate([oa, ob], axis=-1) @ w_out

def odd_layer(hn, w_in, w_out, rel_bias):
    B_, S_, _ = hn.shape
    cq, ck, cv, c_gate = split_cols(hn @ w_in, ODD_SPLITS)
    oc = moba_attention(cq.reshape(B_, S_, MOBA_HEADS, MOBA_DH), ck.reshape(B_, S_, MOBA_KV_HEADS, MOBA_DH),
                        cv.reshape(B_, S_, MOBA_KV_HEADS, MOBA_DH), rel_bias)
    return (oc * jax.nn.silu(c_gate)) @ w_out

def second_inputs(seed: int = 0) -> dict:
    key = jax.random.key(seed)
    ks = jax.random.split(key, 12)
    f32 = jnp.float32
    x = jax.random.normal(ks[0], (BATCH, SEQ, D_MODEL), f32)
    norm_gain = 1.0 + 0.02 * jax.random.normal(ks[1], (DEPTH, D_MODEL), f32)
    final_gain = 1.0 + 0.02 * jax.random.normal(ks[2], (D_MODEL,), f32)
    rel_bias = 0.2 * jax.random.normal(ks[3], (REL_BUCKETS, ATTN_HEADS), f32)
    w_in_even = jax.random.normal(ks[4], (N_EVEN, D_MODEL, EVEN_COLS), f32) * D_MODEL ** -0.5
    gla_w_up = jax.random.normal(ks[5], (N_EVEN, GLA_RANK, GLA_HEADS * GLA_DK), f32) * GLA_RANK ** -0.5
    gla_b_up = 0.1 * jax.random.normal(ks[6], (N_EVEN, GLA_HEADS * GLA_DK), f32)
    gla_norm_gain = 1.0 + 0.02 * jax.random.normal(ks[7], (N_EVEN, GLA_DV), f32)
    swa_sinks = 0.5 * jax.random.normal(ks[8], (N_EVEN, SWA_HEADS), f32)
    w_out_even = jax.random.normal(ks[9], (N_EVEN, EVEN_WIDTH, D_MODEL), f32) * EVEN_WIDTH ** -0.5
    w_in_odd = jax.random.normal(ks[10], (N_ODD, D_MODEL, ODD_COLS), f32) * D_MODEL ** -0.5
    w_out_odd = jax.random.normal(ks[11], (N_ODD, C_WIDTH, D_MODEL), f32) * C_WIDTH ** -0.5
    return {"x": x, "norm_gain": norm_gain, "final_gain": final_gain, "rel_bias": rel_bias,
            "w_in_even": w_in_even, "gla_w_up": gla_w_up, "gla_b_up": gla_b_up,
            "gla_norm_gain": gla_norm_gain, "swa_sinks": swa_sinks, "w_out_even": w_out_even,
            "w_in_odd": w_in_odd, "w_out_odd": w_out_odd}

def second_block(x, norm_gain, final_gain, rel_bias, w_in_even, gla_w_up, gla_b_up, gla_norm_gain,
              swa_sinks, w_out_even, w_in_odd, w_out_odd):
    h = x
    for layer in range(DEPTH):
        hn = rmsnorm_2(h, norm_gain[layer])
        if layer % 2 == 0:
            i = layer // 2
            h = h + even_layer(hn, w_in_even[i], gla_w_up[i], gla_b_up[i], gla_norm_gain[i],
                               swa_sinks[i], w_out_even[i], rel_bias)
        else:
            i = layer // 2
            h = h + odd_layer(hn, w_in_odd[i], w_out_odd[i], rel_bias)
    return rmsnorm_2(h, final_gain)


def setup_inputs(seed=0):
    out = dict(first_inputs(seed))
    for name, value in second_inputs(seed + 1).items():
        if name != "x":
            out[name + "_2"] = value
    return out


def reference(
    x, c, ctx, c_ctx, ada_w, ada_b, norm_mix_g, norm_ffn_g, mla_wq_a, mla_q_a_norm, mla_wq_b,
    mla_wkv_a, mla_kv_a_norm, mla_wkv_b, mla_q_norm, mla_k_norm, mla_wo, gm_w_in, gm_ln_g,
    gm_ln_b, gm_ws, gm_bs, gm_w_out, ffn_w1, ffn_w2, norm_gain_2, final_gain_2, rel_bias_2,
    w_in_even_2, gla_w_up_2, gla_b_up_2, gla_norm_gain_2, swa_sinks_2, w_out_even_2, w_in_odd_2,
    w_out_odd_2,
):
    x = first_block(
        x, c, ctx, c_ctx, ada_w, ada_b, norm_mix_g, norm_ffn_g, mla_wq_a, mla_q_a_norm,
        mla_wq_b, mla_wkv_a, mla_kv_a_norm, mla_wkv_b, mla_q_norm, mla_k_norm, mla_wo, gm_w_in,
        gm_ln_g, gm_ln_b, gm_ws, gm_bs, gm_w_out, ffn_w1, ffn_w2,
    )
    return second_block(
        x, norm_gain_2, final_gain_2, rel_bias_2, w_in_even_2, gla_w_up_2, gla_b_up_2,
        gla_norm_gain_2, swa_sinks_2, w_out_even_2, w_in_odd_2, w_out_odd_2,
    )


_drawn_inputs = setup_inputs


def setup_inputs(seed=0):
    import zlib

    import numpy as np

    out = dict(_drawn_inputs(seed))
    spreads = {}
    factors = {'ctx': 2.887,
     'norm_mix_g': 2.79,
     'mla_q_a_norm': 8.0,
     'mla_kv_a_norm': 8.0,
     'mla_q_norm': 8.0,
     'mla_k_norm': 8.0,
     'gm_ln_g': 4.91,
     'gm_ln_b': 8.0,
     'gm_bs': 4.926,
     'norm_gain_2': 3.822,
     'final_gain_2': 2.902,
     'rel_bias_2': 3.108,
     'gla_b_up_2': 3.451,
     'gla_norm_gain_2': 8.0,
     'swa_sinks_2': 8.0}
    for name, (base, spread) in spreads.items():
        noise = np.random.default_rng([zlib.crc32(name.encode()), seed]).standard_normal(out[name].shape)
        drawn = base * np.exp(spread * noise) if base else spread * noise
        out[name] = __import__('jax').numpy.asarray(drawn.astype(out[name].dtype))
    for name, factor in factors.items():
        out[name] = (out[name] * factor).astype(out[name].dtype)
    return out
```

```python
import numpy as np
from contextlib import ExitStack
import concourse.bass as bass
from concourse import mybir

P = 128
D = 1024
KT = D // P
S = 256
CTX = 256
SC = S + CTX
H = 8
Q_LORA, KV_LORA, ROPE = 384, 256, 64
FFN = 4096
GM = 2048
CW = 1024
RING = 4
ADA_FIRST = 16
QK = 192
TAU = 16.0
EPS = 1e-6
NEG = -1e30
MASKW = 384
ADA_MODS = 10

STAGES = [
    ("q_a", [1] * 3), ("kv_a", [1] * 3), ("q_b", [2] * 6), ("kv_b_k", [4] * 2), ("kv_b_v", [4] * 2),
    ("mla_out", [1] * 8),
    ("ffn0_up", [1] * 32), ("ffn0_down", [0, 0, 0, 1] * 8),
    ("gm_v", [0, 0, 0, 2] * 4), ("gm_u", [1] * 16), ("gm_out", [0, 1] * 8),
    ("ffn1_up", [1] * 32), ("ffn1_down", [0, 0, 0, 1] * 8),
    ("even_a", [1] * 5), ("even_av", [0, 0, 0, 2]), ("even_b", [1] * 14), ("even_out", [1] * 8),
    ("odd_f", [1] * 18), ("odd_v", [0, 2]), ("odd_out", [1] * 8),
]


class Count:

    def __init__(self):
        self.chunk0, self.group0 = {}, {}
        self.after_chunk, self.after_group = [], []
        steps = 0
        for name, ends in STAGES:
            self.chunk0[name] = len(self.after_chunk)
            self.group0[name] = len(self.after_group)
            for n in ends:
                self.after_group += [steps + i + 1 for i in range(n)]
                steps += max(1, n)
                self.after_chunk.append(steps)
        self.chunks, self.groups = len(self.after_chunk), len(self.after_group)


SPLITS = [
    ("mla_in", 16), ("cq", 3), ("ckv", 4), ("mla_o", 8),
    ("ffn0_in", 8), ("ffn0_hid", 32), ("gm_in", 8), ("gm_s", 16), ("ffn1_in", 8), ("ffn1_hid", 32),
    ("even_in", 8), ("even_o", 8), ("odd_in", 8), ("odd_o", 8),
]


def written(i):
    base = split_base()
    return i + 1 - sum(32 for name in ("ffn0_hid", "ffn1_hid") if i > base[name])


def split_base():
    base, n = {}, 0
    for name, k in SPLITS:
        base[name] = n
        n += k
    return base


VECS = [
    ("c", 8), ("c_ctx", 8), ("ada_b0", 48), ("ada_b1", 48), ("norm_mix_g", 16), ("norm_ffn_g", 16),
    ("q_a_norm", 3), ("kv_a_norm", 2), ("q_g_nope", 1), ("q_g_rope", 1), ("k_g_nope", 1),
    ("k_g_rope", 1), ("gm_ln_g", 16), ("gm_ln_b", 16), ("norm_gain_2", 16), ("final_gain", 8), ("gla_b_up", 2), ("gla_gain", 1),
    ("sinks", 8),
]


def vec_offsets():
    at, n = {}, 0
    for name, k in VECS:
        at[name] = (n, n + k)
        n += k
    return at, n


def build_program(nc, vecs, consts, gm_rows, rel_ext, x_in, ctx_in, ada, weights,
                  gm_ws, gla_w_up, out):
    fp32, fp32r = mybir.dt.float32, mybir.dt.float32r
    ALU, ACT, AX = mybir.AluOpType, mybir.ActivationFunctionType, mybir.AxisListType
    ds = bass.ds
    count, split0 = Count(), split_base()
    chunk0, group0 = count.chunk0, count.group0
    after_chunk, after_group = count.after_chunk, count.after_group
    n_chunks = count.chunks
    vec_at, n_vec = vec_offsets()
    scratch = nc.dram_tensor("bias_by_distance", (16, MASKW), fp32, kind="Internal").ap()

    hold = ExitStack()
    with hold:
        def sb(name, shape, dt=fp32, stack=hold):
            return stack.enter_context(nc.sbuf_tensor(name, shape, dt))

        def sem(name):
            return hold.enter_context(nc.semaphore(name))

        x = sb("x", [P, KT, S])
        raw = sb("raw", [P, RING, CW])
        w_hi = sb("w_hi", [P, RING, CW], fp32r)
        w_lo = sb("w_lo", [P, RING, CW], fp32r)
        ada_raw = sb("ada_raw", [P, RING, CW])
        ada_acc = sb("ada_acc", [P, 2, CW])
        vec = sb("vec", [P, n_vec])
        const = sb("const", [P, P + 18])
        silu_c = sb("silu_c", [P, KT, 2])
        mod_in = sb("mod_in", [P, 2 * KT, 2])
        mods = sb("mods", [P, ADA_MODS, KT])
        gain = sb("gain", [P, 5, KT])
        act_hi = sb("act_hi", [P, KT, S], fp32r)
        act_lo = sb("act_lo", [P, KT, S], fp32r)
        tile_f32 = sb("tile_f32", [P, 4, S])
        sq = sb("sq", [P, KT, S])
        std = sb("std", [P, SC])
        rstd = sb("rstd", [P, SC])
        square_sum = sb("square_sum", [P, S])
        eps = sb("eps", [P, 1])
        ones = sb("ones", [P, P])
        mean = sb("mean", [P, P])
        small = sb("small", [P, 96])

        with ExitStack() as mla:
            with ExitStack() as first:
                in_hi = sb("mla_in_hi", [P, KT, SC], fp32r, first)
                in_lo = sb("mla_in_lo", [P, KT, SC], fp32r, first)
            kn = sb("kn", [P, H, SC], fp32, mla)
            v_mla = sb("v_mla", [P, 4, H * P], fp32, mla)
            with ExitStack() as first:
                ctx = sb("ctx", [P, KT, CTX], fp32, first)
                sq_ctx = sb("sq_ctx", [P, KT, CTX], fp32, first)
                ckv = sb("ckv", [P, 2, SC], fp32, first)
                cq = sb("cq", [P, 3, S], fp32, first)
                sq_lora = sb("sq_lora", [P, 3, SC], fp32, first)
            qn = sb("qn", [P, H, S], fp32, mla)
            qr = sb("qr", [P, H // 2, S], fp32, mla)
            kr = sb("kr", [P, H // 2, SC], fp32, mla)
            p_mla = sb("p_mla", [P, 2, SC], fp32, mla)
            pt_mla = sb("pt_mla", [P, 2, 4, S], fp32, mla)
            ckv_hi = sb("ckv_hi", [P, 2, SC], fp32r, mla)
            ckv_lo = sb("ckv_lo", [P, 2, SC], fp32r, mla)
            cq_hi = sb("cq_hi", [P, 3, S], fp32r, mla)
            cq_lo = sb("cq_lo", [P, 3, S], fp32r, mla)
            kpe = sb("kpe", [P, SC], fp32, mla)
            rope = sb("rope", [P, P + 2 * S], fp32, mla)
            q_scale = sb("q_scale", [P, 2, 2, H], fp32, mla)
            gqk = sb("gqk", [P, 1], fp32, mla)
        late = hold.enter_context(ExitStack())
        bias = sb("bias", [P, 16, S], fp32, late)
        anti = sb("anti", [P, P], fp32, late)
        with ExitStack() as ffn:
            hid_hi = sb("hid_hi", [P, FFN // P, S], fp32r, ffn)
            hid_lo = sb("hid_lo", [P, FFN // P, S], fp32r, ffn)
            relu = sb("relu", [P, 2, S], fp32, ffn)
            table = sb("table", [H, 2, MASKW], fp32, ffn)
            onehot = sb("onehot", [33, 2, MASKW], fp32, ffn)
            rel = sb("rel", [33, H], fp32, ffn)
        with ExitStack() as gm:
            v_gm = sb("v_gm", [P, 2, GM], fp32, gm)
            u_gm = sb("u_gm", [P, GM // P, S], fp32, gm)
            s_hi = sb("s_hi", [P, GM // P, S], fp32r, gm)
            s_lo = sb("s_lo", [P, GM // P, S], fp32r, gm)
            ws = sb("ws", [P, 8, P], fp32, gm)
            mix_bias = sb("mix_bias", [P, GM // P // 2, P], fp32, gm)
            ln_stats = sb("ln_stats", [P, 2, 4, 6], fp32, gm)
            ln_mv = sb("ln_mv", [P, 2, 4], fp32, gm)
        with ExitStack() as even:
            masks = sb("masks", [P, 2 * S + P], fp32, even)
            down = sb("down", [16, S], fp32, even)
            w_up = sb("w_up", [16, S], fp32, even)
            aq = sb("aq", [P, 2, S], fp32, even)
            ak = sb("ak", [P, 2, S], fp32, even)
            z = sb("z", [P, 2, S], fp32, even)
            zl = sb("zl", [P, 2, S], fp32, even)
            cum = sb("cum", [P, 2, S], fp32, even)
            e_pos = sb("e_pos", [P, 2, S], fp32, even)
            e_neg = sb("e_neg", [P, 2, S], fp32, even)
            e_last = sb("e_last", [P, 2, S], fp32, even)
            qe = sb("qe", [P, 2, S], fp32, even)
            ke = sb("ke", [P, 2, S], fp32, even)
            kl = sb("kl", [P, 2, S], fp32, even)
            decay = sb("decay", [P, 2, 2, 4], fp32, even)
            kl_tok = sb("kl_tok", [P, 2, 2, P], fp32, even)
            av = sb("av", [P, 2, 512], fp32, even)
            att = sb("att", [P, H, P], fp32, even)
            state = sb("state", [P, 3, 2, P], fp32, even)
            bq = sb("bq", [P, 4, S], fp32, even)
            bk = sb("bk", [P, S], fp32, even)
            bv = sb("bv", [P, S], fp32, even)
            bv_tok = sb("bv_tok", [P, 2, P], fp32, even)
            gate = sb("gate", [P, H, S], fp32, even)
            o_gla = sb("o_gla", [P, 2, S], fp32, even)
            rms_gla = sb("rms_gla", [H, P], fp32, even)
            logit = sb("logit", [P, 2, S], fp32, even)
            prob = sb("prob", [P, 2, S], fp32, even)
            prob_t = sb("prob_t", [P, 4, 2, P], fp32, even)
        with ExitStack() as odd:
            cq_o = sb("cq_o", [P, H, S], fp32, odd)
            ck_o = sb("ck_o", [P, 2, S], fp32, odd)
            cv_o = sb("cv_o", [P, 2, S], fp32, odd)
            gate_o = sb("gate_o", [P, H, S], fp32, odd)
            logit_o = sb("logit_o", [P, 2, S], fp32, odd)
            prob_o = sb("prob_o", [P, 2, S], fp32, odd)
            prob_t_o = sb("prob_t_o", [P, 4, 2, P], fp32, odd)
            result = sb("result", [P, KT, S], fp32, odd)

        bank = [hold.enter_context(nc.psum_tensor(f"bank{i}", [P, 512], fp32)) for i in range(8)]

        def V(name, a=0, n=None):
            lo, hi = vec_at[name]
            return vec[:, lo + a:hi if n is None else lo + a + n]

        ws_sum = sq[:, 0:4, :].rearrange("p a (b c) -> p (a b) c", c=P)
        bs_all = sq[:, 4:8, :].rearrange("p a (b c) -> p (a b) c", c=P)

        def squares_before(norm):
            return 0 if norm == 0 else 8 * (norm + 1)

        def ada_end(m):
            return KT * (m + 1) if m < 4 else KT * (m // 2 * 2 + 2)

        def sq_k(h):
            return sq[:, 2 * (h % 4):2 * (h % 4) + 2, :].rearrange("p a b -> p (a b)")

        ident = const[:, 0:P]
        rot, cos, sin = rope[:, 0:P], rope[:, P:P + S], rope[:, P + S:P + 2 * S]

        mod_rows = pt_mla[0:2].rearrange("p a b c -> p (a b c)")

        def one_column(j):
            return const[:, P + 7 - j:P + 15 - j]

        small_in, x_in_sem, ctx_in_sem, rope_in = sem("small_in"), sem("x_loaded"), sem("ctx_loaded"), sem("rope_in")
        table_in, gm_in, masks_in = sem("table_in"), sem("gm_in"), sem("masks_in")
        raw_in = [sem(f"raw_in{i}") for i in range(RING)]
        ada_in = [sem(f"ada_in{i}") for i in range(RING)]
        weight_hi, weight_lo, matmul_steps = sem("weight_hi"), sem("weight_lo"), sem("matmul_steps")
        evacuated = sem("evacuated")
        split_src, split_hi, split_lo = sem("split_src"), sem("split_hi"), sem("split_lo")
        hid_squared = sem("hid_squared")
        silu_ready, first_used, rows_ready, first_cols = (
            sem(n) for n in ("silu_ready", "first_used", "first_rows_ready", "first_cols"))
        ada_used, ada_cols, mods_ready = sem("ada_used"), sem("ada_cols"), sem("mods_ready")
        setup = sem("setup")
        squared, square_sums, sums_ready, std_ready = (
            sem(n) for n in ("squared", "square_sums", "sums_ready", "std_ready"))
        dve_own, act_own = sem("dve_own"), sem("act_own")
        lora_sums, lora_std, lora_rstd = sem("lora_sums"), sem("lora_std"), sem("lora_rstd")
        q_squared, q_sums, q_sums_read, q_sum_added, q_std, q_ready = (
            sem(n) for n in ("q_squared", "q_sums", "q_sums_read", "q_sum_added", "q_std", "q_ready"))
        pe_gained, rotated, k_squared, k_sums, k_std, k_rstd, k_spread, k_ready = (
            sem(n) for n in ("rope_gained", "rotated", "k_squared", "k_sums", "k_std", "k_rstd",
                             "k_spread", "k_ready"))

        class Attention:

            def __init__(self, name):
                (self.scores, self.logits, self.negmax, self.probs, self.normed, self.turned,
                 self.turned_read, self.values) = (
                    sem(f"{name}_{n}") for n in ("scores", "logits", "negmax", "probs", "normed",
                                                 "turned", "turned_read", "values"))

        latent, window, blocks = Attention("latent"), Attention("window"), Attention("blocks")
        table_sums, table_out, table_stored, table_skewed, bias_turned, bias_ready = (
            sem(n) for n in ("table_sums", "table_out", "table_stored", "table_skewed",
                             "bias_turned", "bias_ready"))
        ln_counted, ln_var, ln_std, v_normed, ws_sums, ws_sum_ready, mixed = (
            sem(n) for n in ("ln_counted", "ln_var", "ln_std", "v_normed", "ws_sums", "ws_sum_ready", "mixed"))
        g_z, g_z_ready, g_ln, g_last, g_exp, g_factors, g_turned, g_tok = (
            sem("gla_" + n) for n in ("z", "z_ready", "ln", "last", "exp", "factors",
                                      "k_turned", "k_tok"))
        g_kv, g_state, g_att, g_att_ready, g_o, g_squared, g_sums, g_std, g_rstd, g_spread = (
            sem("gla_" + n) for n in ("kv", "state", "att", "att_ready", "o", "o_squared",
                                      "o_sums", "o_std", "o_rstd", "o_spread"))
        v_turned, v_tok, att_zero = sem("v_turned"), sem("v_tok"), sem("att_zero")
        out_ready, out_written = sem("out_ready"), sem("out_written")

        block = hold.enter_context(nc.Block())

        def at(value, it, per_body):
            return value if it is None else value + it * per_body

        EPS_SET, MEAN_SET = 2, 3

        @block.sync
        def _(sp):
            def load_weights(c, it=None):
                slot = c % RING
                if it is not None or c >= RING:
                    sp.wait_ge(weight_lo, at(c - RING + 1, it, 8))
                row = c if it is None else ds(c + it * 8, 1)
                src = weights[row] if it is None else weights[row].rearrange("o p n -> (o p) n")
                sp.dma_start(raw[:, slot, :], src).then_inc(raw_in[slot], 16)

            def load_ada(a, it=None):
                slot = a % RING
                if it is not None or a >= RING:
                    sp.wait_ge(ada_used, at(a - RING + 1, it, 4))
                else:
                    sp.wait_ge(first_used, ADA_FIRST - RING + 1 + a)
                a += ADA_FIRST
                src = ada[a] if it is None else ada[ds(a + it * 4, 1)].rearrange("o p n -> (o p) n")
                sp.dma_start(ada_raw[:, slot, :], src).then_inc(ada_in[slot], 16)

            sp.dma_start(vec[:], vecs).then_inc(small_in, 16)
            sp.dma_start(const[:], consts["const"]).then_inc(small_in, 16)
            for o in range(ADA_FIRST):
                if o >= RING:
                    sp.wait_ge(first_used, o - RING + 1)
                sp.dma_start(ada_raw[:, o % RING, :], ada[o]).then_inc(ada_in[o % RING], 16)
                if o == 9:
                    sp.dma_start(x[:], x_in).then_inc(x_in_sem, 16)
            load_weights(0)
            load_weights(1)
            sp.dma_start(ctx[:], ctx_in).then_inc(ctx_in_sem, 16)
            load_weights(2)
            load_weights(3)
            sp.dma_start(rope[:], consts["rope"]).then_inc(rope_in, 16)
            for c in range(4, 8):
                load_weights(c)
            for a in range(32):
                load_ada(a)
                if a < 16:
                    load_weights(8 + a)
            sp.wait_ge(latent.values, H)
            sp.dma_start(onehot[:], consts["onehot"]).then_inc(table_in, 16)
            sp.dma_start(rel[:], rel_ext).then_inc(table_in, 16)
            sp.dma_start(anti[:], consts["anti"]).then_inc(table_in, 16)
            for c in range(24, 28):
                load_weights(c)
            sp.wait_ge(table_out, 1)
            sp.dma_start(scratch.rearrange("(t h) d -> h t d", t=2), table[:]).then_inc(table_stored, 16)
            sp.wait_ge(table_stored, 16)
            skewed = bass.AP(scratch.tensor, 0, [[1, P], [MASKW, 16], [1, S]])
            sp.dma_start(bias[:], skewed).then_inc(table_skewed, 16)
            with sp.Fori(0, 12) as it:
                for j in range(8):
                    if j % 2 == 0:
                        load_ada(32 + j // 2, it)
                    load_weights(28 + j, it)
            c = 124
            with sp.Fori(0, (count.chunks - c) // 8) as it:
                for j in range(8):
                    load_weights(c + j, it)
            c += (count.chunks - c) // 8 * 8
            for c in range(c, count.chunks):
                load_weights(c)
            sp.wait_ge(out_ready, KT)
            sp.dma_start(out, result[:]).then_inc(out_written, 16)
            sp.wait_ge(out_written, 16)

        @block.tensor
        def _(pe):
            def split_product(dst, w, a, start, stop, weights_move=False):
                if weights_move:
                    w, a = a, w
                pe.matmul(dst, w[0], a[0], start=start, stop=False)
                pe.matmul(dst, w[0], a[1], start=False, stop=False)
                return pe.matmul(dst, w[1], a[0], start=False, stop=stop)

            def weight(c, col, width):
                slot = c % RING
                return w_hi[:, slot, col:col + width], w_lo[:, slot, col:col + width]

            def project(name, k_tiles, a, width=S, tiles=KT, locals_=None, it=None, per=0, a_wait=None):
                c0, n0 = chunk0[name], group0[name]
                for i in (range(len(dict(STAGES)[name])) if locals_ is None else locals_):
                    pe.wait_ge(weight_lo, at(c0 + i + 1, it, 8))
                    for t in range(tiles):
                        g, k = divmod(i * tiles + t, k_tiles)
                        n = n0 + g
                        if k == 0 and n >= 2:
                            pe.wait_ge(evacuated, at(n - 1, it, per))
                        if g == 0 and a_wait is not None:
                            pe.wait_ge(split_lo, a_wait(k))
                        last = split_product(bank[n % 2][:, 0:width], weight(c0 + i, t * P, P), a(k),
                                             k == 0, k == k_tiles - 1)
                        if k == k_tiles - 1 or t == tiles - 1:
                            last.then_inc(matmul_steps, 1)
                    yield i

            def run(stage):
                for _ in stage:
                    pass

            def project_tokens(name, chunks, banks, a, k_chunk, width, it=None, groups=(), a_wait=None):
                c0 = chunk0[name]
                k_all = k_chunk * len(chunks)
                for x_, i in enumerate(chunks):
                    pe.wait_ge(weight_lo, at(c0 + i + 1, it, 8))
                    for tt in range(2):
                        if x_ == 0:
                            pe.wait_ge(evacuated, groups[tt])
                        for kk in range(k_chunk):
                            k = x_ * k_chunk + kk
                            if tt == 0 and a_wait is not None:
                                pe.wait_ge(split_lo, a_wait(k))
                            hi, lo = a(k)
                            last = split_product(
                                bank[banks[tt]][:, 0:width], weight(c0 + i, kk * width, width),
                                (hi[:, tt * P:(tt + 1) * P], lo[:, tt * P:(tt + 1) * P]),
                                k == 0, k == k_all - 1, weights_move=True)
                        if tt == 1 or x_ == len(chunks) - 1:
                            last.then_inc(matmul_steps, 1)

            def act(k):
                return act_hi[:, k, :], act_lo[:, k, :]

            def sum_squares(norm):
                pe.wait_ge(square_sums, (norm + 1) * (KT - 2))
                pe.matmul(bank[4][:, 0:S], mean[:], square_sum[:], start=True, stop=False)
                pe.wait_ge(squared, squares_before(norm) + KT)
                pe.matmul(bank[4][:, 0:S], mean[:], sq[:, KT - 1, :], start=False, stop=True).then_inc(sums_ready, 1)

            def modulation_column(m, o):
                return pe.matmul(bank[7][:, (m % 2) * KT + o:(m % 2) * KT + o + 1],
                                 ada_acc[:, m % 2, o * P:(o + 1) * P], ones[:, 0:1], start=True, stop=True)

            def modulation_columns(mods_):
                if not mods_:
                    return
                pe.wait_ge(ada_used, ada_end(mods_[-1]))
                if mods_[0] >= 1:
                    pe.wait_ge(mods_ready, mods_[0])
                for m in mods_:
                    for o in range(KT):
                        last = modulation_column(m, o)
                last.then_inc(ada_cols, len(mods_))

            def first_columns(m):
                pe.wait_ge(rows_ready, m + 1)
                for o in range(m * KT, (m + 1) * KT):
                    last = pe.matmul(bank[7][:, 2 * o:2 * o + 2], mod_rows[:, o * P:(o + 1) * P],
                                     ident[0:2, 0:2], start=True, stop=True)
                last.then_inc(first_cols, 1)

            pe.wait_ge(small_in, 32)
            pe.wait_ge(silu_ready, 2)
            for o in range(ADA_FIRST):
                m, k = divmod(o, KT)
                pe.wait_ge(ada_in[o % RING], 16 * (o // RING + 1))
                for half in range(2):
                    last = pe.matmul(bank[2 * m + half][0:2, :], silu_c[:, k, :],
                                     ada_raw[:, o % RING, half * 512:(half + 1) * 512],
                                     start=k == 0, stop=k == KT - 1)
                last.then_inc(first_used, 1)
                if o == 11:
                    first_columns(0)
            pe.wait_ge(setup, MEAN_SET)
            sum_squares(0)
            first_columns(1)
            for k in range(KT):
                pe.wait_ge(squared, KT + k + 1)
                last = pe.matmul(bank[5][:, 0:CTX], mean[:], sq_ctx[:, k, :], start=k == 0, stop=k == KT - 1)
            last.then_inc(sums_ready, 1)

            run(project("q_a", 8, lambda k: (in_hi[:, k, CTX:SC], in_lo[:, k, CTX:SC]),
                        a_wait=lambda k: k + 1))
            stage = project("kv_a", 8, lambda k: (in_hi[:, k, :], in_lo[:, k, :]), width=SC,
                            a_wait=lambda k: KT + k + 1)
            next(stage)
            pe.wait_ge(evacuated, group0["q_a"] + 3)
            for k in range(3):
                last = pe.matmul(bank[4][:, 0:S], ones[:], sq[:, k, :], start=k == 0, stop=k == 2)
            last.then_inc(lora_sums, 1)
            run(stage)
            pe.wait_ge(evacuated, group0["kv_a"] + 3)
            for k in range(2):
                last = pe.matmul(bank[5][:], ones[:], sq_lora[:, k, :], start=k == 0, stop=k == 1)
            last.then_inc(lora_sums, 1)
            pe.matmul(bank[2][0:H, :], ones[0:ROPE, 0:H], sq_lora[0:ROPE, 2, :], start=True, stop=False)

            def query_sums(i):
                pe.wait_ge(q_squared, i + 1)
                n, col, sel = (1, i, ones[:, 0:1]) if i < H else (2, H + 2 * (i - H), const[:, P + 16:P + 18])
                for qt in range(2):
                    at_ = qt * 2 * H + col
                    last = pe.matmul(bank[6][:, at_:at_ + n], sq[:, i % 8, qt * P:(qt + 1) * P], sel,
                                     start=True, stop=True)
                last.then_inc(q_sums, 1)

            stage = project("q_b", 3, lambda k: (cq_hi[:, k, :], cq_lo[:, k, :]), tiles=6,
                            a_wait=lambda k: split0["cq"] + k + 1)
            for i in stage:
                if i > 0:
                    query_sums(2 * i - 2)
                    query_sums(2 * i - 1)
            query_sums(10)
            query_sums(11)
            modulation_columns([0])
            run(project("kv_b_k", 2, lambda k: (ckv_hi[:, k, :], ckv_lo[:, k, :]), width=SC,
                        a_wait=lambda k: split0["ckv"] + 4))
            pe.wait_ge(rope_in, 16)
            for p_ in range(4):
                pe.wait_ge(pe_gained, p_ + 1)
                pe.matmul(bank[4 + p_ // 2][:, (p_ % 2) * S:(p_ % 2 + 1) * S], rot, qr[:, p_, :],
                          start=True, stop=True).then_inc(rotated, 1)
            pe.wait_ge(pe_gained, 5)
            pe.matmul(bank[3][:, 0:S], rot, kpe[:, CTX:SC], start=True, stop=True).then_inc(rotated, 1)
            for h in range(H):
                pe.wait_ge(k_squared, h + 1)
                pe.matmul(bank[2][0:H, :], one_column(h), sq_k(h), start=False,
                          stop=h == H - 1).then_inc(k_sums, 1)
            for i in range(2):
                c, n0 = chunk0["kv_b_v"] + i, group0["kv_b_v"] + 4 * i
                pe.wait_ge(weight_lo, c + 1)
                for tt in range(4):
                    tok = slice(tt * P, (tt + 1) * P)
                    pe.wait_ge(evacuated, n0 + tt - 1)
                    for k in range(2):
                        last = split_product(bank[(n0 + tt) % 2][:], weight(c, k * 512, 512),
                                             (ckv_hi[:, k, tok], ckv_lo[:, k, tok]), k == 0, k == 1,
                                             weights_move=True)
                    last.then_inc(matmul_steps, 1)

            def key_spread(h):
                if h < 2:
                    pe.wait_ge(evacuated, group0["kv_b_v"] + 8)
                else:
                    pe.wait_ge(k_ready, h - 1)
                pe.matmul(bank[h % 2][:], ident[0:H, h:h + 1].to_broadcast([H, P]), rstd[0:H, :],
                          start=True, stop=True).then_inc(k_spread, 1)

            def latent_scores(u):
                h, qt = divmod(u, 2)
                r = slice((h % 2) * ROPE, (h % 2 + 1) * ROPE)
                tok = slice(qt * P, (qt + 1) * P)
                pe.wait_ge(k_ready, h + 1)
                if u >= 2:
                    pe.wait_ge(latent.probs, u - 1)
                pe.matmul(bank[4 + u % 2][:], qn[:, h, tok], kn[:, h, :], start=True, stop=False)
                pe.matmul(bank[4 + u % 2][:], qr[r, h // 2, tok], kr[r, h // 2, :],
                          start=False, stop=True).then_inc(latent.scores, 1)

            def latent_turn(u):
                pe.wait_ge(latent.normed, u + 1)
                if u == 1:
                    pe.wait_ge(mods_ready, 2)
                if u >= 2:
                    pe.wait_ge(latent.turned_read, u - 1)
                for kt in range(4):
                    last = pe.transpose(bank[6 + u % 2][:, kt * P:(kt + 1) * P],
                                        p_mla[:, u % 2, kt * P:(kt + 1) * P], ident)
                last.then_inc(latent.turned, 1)

            def latent_values(h):
                pe.wait_ge(latent.turned_read, 2 * h + 2)
                if h >= 2:
                    pe.wait_ge(split_src, split0["mla_o"] + h - 1)
                for kt in range(4):
                    last = pe.matmul(bank[2 + h % 2][:, 0:S], v_mla[:, kt, h * P:(h + 1) * P],
                                     pt_mla[:, h % 2, kt, :], start=kt == 0, stop=kt == 3)
                last.then_inc(latent.values, 1)

            pe.wait_ge(k_rstd, 1)
            key_spread(0)
            key_spread(1)
            pe.wait_ge(q_ready, 1)
            latent_scores(0)
            latent_scores(1)
            for u in range(2 * H):
                if u % 2 == 0 and u // 2 + 2 < H:
                    key_spread(u // 2 + 2)
                if u + 2 < 2 * H:
                    latent_scores(u + 2)
                latent_turn(u)
                if u == 0:
                    modulation_columns([1])
                if u % 2 == 0 and u > 0:
                    latent_values(u // 2 - 1)
            latent_values(H - 1)
            modulation_columns([2])
            run(project("mla_out", 8, act, a_wait=lambda k: split0["mla_o"] + k + 1))

            pe.wait_ge(table_in, 48)
            for t in range(2):
                pe.matmul(bank[5 + t][0:H, 0:MASKW], rel[:], onehot[:, t, :],
                          start=True, stop=True).then_inc(table_sums, 1)
            sum_squares(1)
            modulation_columns([3])

            def turn_biases(part):
                if part == 0:
                    pe.wait_ge(table_skewed, 16)
                for i in (2 * part, 2 * part + 1):
                    pe.matmul(bank[5 + i % 2][:], anti[:], bias[:, 2 * i:2 * i + 2, :],
                              start=True, stop=True).then_inc(bias_turned, 1)

            def ffn(up, down_, split, norm, mods_up, mods_down):
                hidden = split0[split + "_hid"]
                with pe.Fori(0, 4) as it:
                    run(project(up, 8, act, locals_=range(8), it=it, per=8,
                                a_wait=lambda k: split0[split + "_in"] + k + 1))
                modulation_columns(mods_up)
                with pe.Fori(0, 4) as it:
                    run(project(down_, 32, lambda k: (hid_hi[:, k, :], hid_lo[:, k, :]),
                                locals_=range(8), it=it, per=2, a_wait=lambda k: hidden + k + 1))
                sum_squares(norm)
                modulation_columns(mods_down)
                turn_biases(norm - 2)

            ffn("ffn0_up", "ffn0_down", "ffn0", 2, [4, 5], [6, 7])

            with pe.Fori(0, 2) as it:
                for b in range(2):
                    n = group0["gm_v"] + 2 * b
                    project_tokens("gm_v", range(4 * b, 4 * b + 4), (3 - 2 * b - 1, 3 - 2 * b), act, 2, 512,
                                   it=it, groups=(at(n - 2, it, 4), at(n - 2, it, 4)),
                                   a_wait=(lambda k: split0["gm_in"] + k + 1) if b == 0 else None)
            pe.wait_ge(gm_in, 32)
            pe.wait_ge(mods_ready, 8)
            pe.wait_ge(bias_ready, 2)
            for i in range(2):
                pe.matmul(bank[6 + i][:], ones[:], ws[:, 4 * i:4 * i + 4, :], start=True,
                          stop=True).then_inc(ws_sums, 1)
            with pe.Fori(0, 2) as it:
                run(project("gm_u", 8, act, locals_=range(8), it=it, per=8))
            pe.wait_ge(v_normed, 2)
            pe.wait_ge(ws_sum_ready, 2)
            pe.wait_ge(ada_used, ada_end(9))
            for t in range(GM // P):
                if t >= 2:
                    pe.wait_ge(split_src, written(split0["gm_s"] + t - 2))
                for n in range(2):
                    last = pe.matmul(bank[4 + t % 2][:, n * P:(n + 1) * P], v_gm[:, n, t * P:(t + 1) * P],
                                     ws[:, t // 2, :], start=True, stop=True)
                last.then_inc(mixed, 1)
                if t < KT:
                    last = modulation_column(8, t)
                    if t == KT - 1:
                        last.then_inc(ada_cols, 1)
            with pe.Fori(0, 2) as it:
                run(project("gm_out", 16, lambda k: (s_hi[:, k, :], s_lo[:, k, :]), locals_=range(8),
                            it=it, per=4, a_wait=lambda k: split0["gm_s"] + k + 1))
            sum_squares(3)
            modulation_columns([9])
            turn_biases(1)
            ffn("ffn1_up", "ffn1_down", "ffn1", 4, [], [])

            def scores(att_, heads, u):
                h, qt = divmod(u, 2)
                q, k_, _ = heads(h)
                if u >= 2:
                    pe.wait_ge(att_.logits, u - 1)
                pe.matmul(bank[4 + u % 2][:, 0:(qt + 1) * P], q[:, qt * P:(qt + 1) * P],
                          k_[:, 0:(qt + 1) * P], start=True, stop=True).then_inc(att_.scores, 1)

            def turn(att_, u, src):
                pe.wait_ge(att_.normed, u + 1)
                if u >= 2:
                    pe.wait_ge(att_.turned_read, u - 1)
                for kt in range(u % 2 + 1):
                    last = pe.transpose(bank[6 + u % 2][:, kt * P:(kt + 1) * P],
                                        src[:, u % 2, kt * P:(kt + 1) * P], ident)
                last.then_inc(att_.turned, 1)

            def values(att_, heads, h, turned, part, slot, bank_free):
                pe.wait_ge(att_.turned_read, 2 * h + 2)
                pe.wait_ge(split_src, written(bank_free - 1))
                v = heads(h)[2]
                for qt in range(2):
                    for kt in range(qt + 1):
                        last = pe.matmul(bank[2 + slot % 2][part, qt * P:(qt + 1) * P], v(kt),
                                         turned[:, (2 * h + qt) % 4, kt, :], start=kt == 0, stop=kt == qt)
                last.then_inc(att_.values, 1)

            def even_in(k):
                return split0["even_in"] + k + 1

            run(project("even_a", 8, act, a_wait=even_in))
            n = group0["even_av"]
            pe.wait_ge(masks_in, 32)
            pe.wait_ge(evacuated, n - 4)
            pe.wait_ge(bias_ready, 6)
            for t in range(2):
                pe.matmul(bank[4][:, t * S:(t + 1) * S], w_up[:, t * P:(t + 1) * P], down[:],
                          start=True, stop=True).then_inc(g_z, 1)
            project_tokens("even_av", range(4), (2, 3), act, 2, 512, groups=(n - 2, n - 2))
            stage = project("even_b", 8, act)
            for i in stage:
                if i == 7:
                    pe.wait_ge(evacuated, group0["even_b"] + 6)
                    for tt in range(2):
                        pe.transpose(bank[2][:, tt * P:(tt + 1) * P], bv[:, tt * P:(tt + 1) * P],
                                     ident).then_inc(v_turned, 1)
                    pe.wait_ge(g_factors, 1)
                    for tt in range(2):
                        for p_ in range(2):
                            last = pe.transpose(bank[5][:, (2 * tt + p_) * P:(2 * tt + p_ + 1) * P],
                                                kl[:, p_, tt * P:(tt + 1) * P], ident)
                    last.then_inc(g_turned, 1)

            def pair(h):
                return slice((h % 2) * 64, (h % 2 + 1) * 64)

            pe.wait_ge(v_tok, 1)
            for tt in range(2):
                for h in range(4):
                    at_ = (2 * tt + h // 2) * P
                    pe.matmul(bank[2 + h % 2][:, at_:at_ + P], ke[pair(h), h // 2, tt * P:(tt + 1) * P],
                              qe[pair(h), h // 2, tt * P:(tt + 1) * P], start=True,
                              stop=True).then_inc(g_att, 1)
            pe.wait_ge(g_tok, 1)
            for n in range(3):
                rows = slice((n % 2) * 64, (n % 2 + 1) * 64)
                for h in range(4):
                    at_ = (n // 2) * S + (h // 2) * P
                    last = pe.matmul(bank[6 + n % 2][pair(h), at_:at_ + P],
                                     kl_tok[rows, n // 2, h // 2, (h % 2) * 64:(h % 2 + 1) * 64],
                                     av[rows, n // 2, h * P:(h + 1) * P], start=True, stop=True)
                last.then_inc(g_kv, 1)
            pe.wait_ge(g_att_ready, 2)
            pe.wait_ge(g_state, 3)
            for h in range(4):
                for tt in range(2):
                    tok = slice((h // 2) * S + tt * P, (h // 2) * S + (tt + 1) * P)
                    last = pe.matmul(bank[4 + h % 2][:, tok], av[:, tt, h * P:(h + 1) * P],
                                     att[:, (h % 2) * 4 + 2 * tt + h // 2, :], start=True, stop=False)
                    for n in (2 * tt, 2 * tt + 1):
                        if n > 0:
                            at_ = (h // 2) * S + n * 64
                            last = pe.matmul(bank[4 + h % 2][:, at_:at_ + 64], state[pair(h), n - 1, h // 2, :],
                                             qe[pair(h), h // 2, n * 64:(n + 1) * 64], start=False,
                                             stop=n == 2 * tt + 1)
                last.then_inc(g_o, 1)
            for row in range(H):
                h, tt = divmod(row, 2)
                pe.wait_ge(g_squared, h + 1)
                last = pe.matmul(bank[6][0:H, 0:P], one_column(row), sq[:, h, tt * P:(tt + 1) * P],
                                 start=row == 0, stop=row == H - 1)
            last.then_inc(g_sums, 1)
            pe.wait_ge(g_rstd, 1)
            for row in range(H):
                h, tt = divmod(row, 2)
                at_ = (h % 2) * S + tt * P
                pe.matmul(bank[6 + h // 2][:, at_:at_ + P], ident[0:H, row:row + 1].to_broadcast([H, P]),
                          rms_gla[0:H, :], start=True, stop=True).then_inc(g_spread, 1)

            def window_heads(h):
                r = pair(h)
                return bq[r, h // 2, :], bk[r, :], lambda kt: bv_tok[:, kt, (h % 2) * 64:(h % 2 + 1) * 64]

            def attention(att_, heads, probs, turned, part, paired, i0):
                scores(att_, heads, 0)
                scores(att_, heads, 1)
                for u in range(2 * H):
                    if u + 2 < 2 * H:
                        scores(att_, heads, u + 2)
                    turn(att_, u, probs)
                    if u % 2 == 0 and u > 0:
                        value_step(att_, heads, u // 2 - 1, turned, part, paired, i0)
                value_step(att_, heads, H - 1, turned, part, paired, i0)

            def value_step(att_, heads, h, turned, part, paired, i0):
                slot = h // 2 if paired else h
                values(att_, heads, h, turned, part(h), slot, i0 + max(slot - 1, 0))

            pe.wait_ge(split_src, written(split0["even_o"] + 3))
            attention(window, window_heads, prob, prob_t, pair, True, split0["even_o"] + 4)
            run(project("even_out", 8, act, a_wait=lambda k: split0["even_o"] + k + 1))
            sum_squares(5)
            turn_biases(3)

            run(project("odd_f", 8, act, a_wait=lambda k: split0["odd_in"] + k + 1))
            n = group0["odd_v"]
            project_tokens("odd_v", range(2), (2, 3), act, 4, S, groups=(n - 2, n - 2))

            def block_heads(h):
                return cq_o[:, h, :], ck_o[:, h // 4, :], lambda kt: cv_o[:, kt, (h // 4) * P:(h // 4 + 1) * P]

            pe.wait_ge(evacuated, group0["odd_v"] + 2)
            pe.wait_ge(bias_ready, 8)
            attention(blocks, block_heads, prob_o, prob_t_o, lambda h: slice(0, P), False, split0["odd_o"])
            run(project("odd_out", 8, act, a_wait=lambda k: split0["odd_o"] + k + 1))
            sum_squares(6)

        @block.scalar
        def _(act):
            def convert(c, it=None, per=0):
                if c >= n_chunks:
                    return
                slot = c % RING
                act.wait_ge(raw_in[slot], at(16 * (1 + c // RING), it, 32))
                if c >= RING:
                    act.wait_ge(matmul_steps, at(after_chunk[c - RING], it, per))
                act.activation(w_hi[:, slot, :], raw[:, slot, :], ACT.Copy).then_inc(weight_hi, 1)

            def split(i, hi):
                act.wait_ge(split_src, written(i))
                act.activation(hi, tile_f32[:, i % 4, :], ACT.Copy).then_inc(split_hi, 1)

            def evacuate(name, g, dst, func=ACT.Copy, width=S, it=None, steps=0, bank_=None, square=None):
                n = group0[name] + g
                src = bank[n % 2 if bank_ is None else bank_][:, 0:width]
                act.wait_ge(matmul_steps, at(after_group[n], it, steps))
                if square is not None:
                    act.activation(square, src, ACT.Square)
                act.activation(dst, src, func).then_inc(evacuated, 1)

            def root(dst, src, n, wait, value, done):
                act.wait_ge(wait, value)
                act.activation(dst, src, ACT.Sqrt, scale=1.0 / n, bias=eps[0:dst.shape[0], :]).then_inc(done, 1)

            def square_residual(name, k, it=None, groups=0):
                act.wait_ge(evacuated, at(group0[name] + k + 1, it, groups))
                o = k if it is None else ds(it * groups + k, 1)
                act.activation(sq[:, o, :], x[:, o, :], ACT.Square).then_inc(squared, 1)

            act.wait_ge(small_in, 32)
            act.activation(silu_c[:, :, 0], V("c"), ACT.Silu).then_inc(silu_ready, 1)
            act.activation(silu_c[:, :, 1], V("c_ctx"), ACT.Silu).then_inc(silu_ready, 1)
            act.wait_ge(setup, EPS_SET)
            act.wait_ge(x_in_sem, 16)
            for k in range(KT):
                act.activation(sq[:, k, :], x[:, k, :], ACT.Square).then_inc(squared, 1)
            root(std[:, CTX:SC], bank[4][:, 0:S], 1, sums_ready, 1, std_ready)

            convert(0)
            act.wait_ge(ctx_in_sem, 16)
            for k in range(KT):
                act.activation(sq_ctx[:, k, :], ctx[:, k, :], ACT.Square).then_inc(squared, 1)
            for k in range(KT):
                split(k, in_hi[:, k, CTX:SC])
                if k == 1:
                    convert(1)
                if k == 3:
                    root(std[:, 0:CTX], bank[5][:, 0:CTX], 1, sums_ready, 2, std_ready)
            convert(2)
            convert(3)
            for g in range(3):
                for k in range(3 * g, min(3 * g + 3, KT)):
                    split(KT + k, in_hi[:, k, 0:CTX])
                evacuate("q_a", g, cq[:, g, :], square=sq[:, g, :])
                convert(g + 4)
            evacuate("kv_a", 0, ckv[:, 0, :], width=SC, square=sq_lora[:, 0, :])
            convert(7)
            root(std[:, CTX:SC], bank[4][:, 0:S], Q_LORA, lora_sums, 1, lora_std)
            for k in range(3):
                split(split0["cq"] + k, cq_hi[:, k, :])
            evacuate("kv_a", 1, ckv[:, 1, :], width=SC, square=sq_lora[:, 1, :])
            convert(8)
            evacuate("kv_a", 2, kpe[:], width=SC, square=sq_lora[:, 2, :])
            convert(9)
            root(std[:], bank[5][:], KV_LORA, lora_sums, 2, lora_std)
            for i in range(6):
                for g in (2 * i, 2 * i + 1):
                    evacuate("q_b", g, qn[:, g, :] if g < H else qr[:, g - H, :])
                convert(chunk0["q_b"] + i + 4)
                if i == 0:
                    for k in range(4):
                        split(split0["ckv"] + k, ckv_hi[:, k // 2, (k % 2) * S:(k % 2 + 1) * S])
            act.wait_ge(q_sums, 12)
            act.activation(small[:, 0:32], bank[6][:, 0:32], ACT.Copy).then_inc(q_sums_read, 1)
            for i in range(2):
                for g in range(4 * i, 4 * i + 4):
                    evacuate("kv_b_k", g, kn[:, g, :], width=SC)
                convert(chunk0["kv_b_k"] + i + 4)
            root(q_scale[:, 0, :, :], small[:, 32:48].rearrange("p (q h) -> p q h", q=2),
                 QK, q_sum_added, 1, q_std)
            root(std[0:H, :], bank[2][0:H, :], QK, k_sums, H, k_std)
            for i in range(2):
                for tt in range(4):
                    evacuate("kv_b_v", 4 * i + tt, v_mla[:, tt, i * 512:(i + 1) * 512], width=512)
                convert(chunk0["kv_b_v"] + i + 4)
            for u in range(2 * H):
                h, qt = divmod(u, 2)
                act.wait_ge(latent.negmax, u + 1)
                if u >= 2:
                    act.wait_ge(latent.turned, u - 1)
                act.activation(p_mla[:, u % 2, :], bank[4 + u % 2][:], ACT.Exp, bias=small[:, 48 + u:49 + u],
                               scale=q_scale[:, 0, qt, h:h + 1],
                               accum_out=small[:, 64 + u:65 + u]).then_inc(latent.probs, 1)
                for v in ([u - 1] if u > 0 else []) + ([u] if u == 2 * H - 1 else []):
                    hv, qv = divmod(v, 2)
                    act.wait_ge(latent.turned, v + 1)
                    if hv >= 2:
                        act.wait_ge(latent.values, hv - 1)
                    act.activation(pt_mla[:, hv % 2, :, qv * P:(qv + 1) * P],
                                   bank[6 + v % 2][:].rearrange("p (k q) -> p k q", k=4),
                                   ACT.Copy).then_inc(latent.turned_read, 1)
                if u % 2 == 1 and h >= 2:
                    split(split0["mla_o"] + h - 2, act_hi[:, h - 2, :])
            for h in (H - 2, H - 1):
                split(split0["mla_o"] + h, act_hi[:, h, :])
            def output_projection(name):
                for g in range(KT):
                    if g > 0:
                        square_residual(name, g - 1)
                    convert(chunk0[name] + g + 4)
                square_residual(name, KT - 1)

            output_projection("mla_out")

            def bias_part(part):
                for i in (2 * part, 2 * part + 1):
                    act.wait_ge(bias_turned, i + 1)
                    act.activation(bias[:, 2 * i:2 * i + 2, :],
                                   bank[5 + i % 2][:].rearrange("p (a b) -> p a b", a=2),
                                   ACT.Copy).then_inc(bias_ready, 1)

            def norm(number, name):
                root(std[:, 0:S], bank[4][:, 0:S], 1, sums_ready, number + 2, std_ready)
                for k in range(KT):
                    split(split0[name] + k, act_hi[:, k, :])

            def ffn(stage):
                up, down_ = stage + "_up", stage + "_down"
                with act.Fori(0, 4) as it:
                    for g in range(8):
                        n = group0[up] + g
                        i = split0[stage + "_hid"] + g
                        convert(chunk0[up] + g + 4, it, 8)
                        act.wait_ge(split_lo, at(i - 1, it, 8))
                        evacuate(up, g, relu[:, g % 2, :], ACT.Relu, it=it, steps=8)
                        act.wait_ge(evacuated, at(n + 1, it, 8))
                        act.activation(hid_hi[:, ds(it * 8 + g, 1), :], relu[:, g % 2, :],
                                       ACT.Square).then_inc(split_hi, 1)
                with act.Fori(0, 4) as it:
                    for j in range(8):
                        convert(chunk0[down_] + j + 4, it, 8)
                        if j % 4 == 3:
                            square_residual(down_, j // 4, it, 2)

            for t in range(2):
                act.wait_ge(table_sums, t + 1)
                last = act.activation(table[:, t, :], bank[5 + t][0:H, 0:MASKW], ACT.Copy)
            last.then_inc(table_out, 1)
            norm(1, "ffn0_in")
            ffn("ffn0")

            norm(2, "gm_in")
            bias_part(0)
            with act.Fori(0, 2) as it:
                for b in range(2):
                    for j in range(4):
                        if j == 3:
                            for tt in range(2):
                                evacuate("gm_v", 2 * b + tt, v_gm[:, tt, ds(it * 1024 + b * 512, 512)], ACT.Gelu,
                                         width=512, it=it, steps=10, bank_=2 * ((b + 1) % 2) + tt)
                        convert(chunk0["gm_v"] + 4 * b + j + 4, it, 10)
            for tt in range(2):
                act.wait_ge(ln_var, tt + 1)
                act.activation(ln_mv[:, tt, 2:3], ln_mv[:, tt, 1:2], ACT.Sqrt, bias=eps[:]).then_inc(ln_std, 1)
            for i in range(2):
                act.wait_ge(ws_sums, i + 1)
                act.activation(ws_sum[:, 4 * i:4 * i + 4, :], bank[6 + i][:].rearrange("p (a b) -> p a b", a=4),
                               ACT.Copy).then_inc(ws_sum_ready, 1)
            with act.Fori(0, 2) as it:
                for g in range(8):
                    evacuate("gm_u", g, u_gm[:, ds(it * 8 + g, 1), :], ACT.Gelu, it=it, steps=8)
                    convert(chunk0["gm_u"] + g + 4, it, 8)
            for t in range(GM // P):
                split(split0["gm_s"] + t, s_hi[:, t, :])
            with act.Fori(0, 2) as it:
                for j in range(8):
                    convert(chunk0["gm_out"] + j + 4, it, 8)
                    if j % 2 == 1:
                        square_residual("gm_out", j // 2, it, 4)

            norm(3, "ffn1_in")
            bias_part(1)
            ffn("ffn1")

            norm(4, "even_in")
            bias_part(2)
            for g, dst in enumerate([down[:], aq[:, 0, :], aq[:, 1, :], ak[:, 0, :], ak[:, 1, :]]):
                if g == 0:
                    n = group0["even_a"]
                    act.wait_ge(matmul_steps, after_group[n])
                    act.activation(dst, bank[n % 2][0:16, 0:S], ACT.Copy).then_inc(evacuated, 1)
                else:
                    evacuate("even_a", g, dst)
                convert(chunk0["even_a"] + g + 4)
            act.wait_ge(g_z_ready, 2)
            act.activation(zl[:], z[:], ACT.Abs).then_inc(act_own, 1)
            act.wait_ge(act_own, 1)
            act.activation(zl[:], zl[:], ACT.Exp, scale=-1.0).then_inc(act_own, 1)
            act.wait_ge(act_own, 2)
            act.activation(zl[:], zl[:], ACT.Ln, bias=1.0).then_inc(g_ln, 1)
            for j in range(4):
                if j == 3:
                    for tt in range(2):
                        evacuate("even_av", tt, av[:, tt, :], width=512, bank_=2 + tt)
                convert(chunk0["even_av"] + j + 4)
            act.wait_ge(g_last, 1)
            act.activation(e_pos[:], cum[:], ACT.Exp, scale=1.0 / TAU)
            act.activation(e_neg[:], cum[:], ACT.Exp, scale=-1.0 / TAU)
            act.activation(decay[:, 1], decay[:, 0], ACT.Exp)
            for t in range(2):
                for n in range(4):
                    tok = slice(n * 64, (n + 1) * 64)
                    ins = act.activation(e_last[:, t, tok], cum[:, t, tok], ACT.Exp, scale=-1.0 / TAU,
                                         bias=decay[:, 0, t, n:n + 1])
            ins.then_inc(g_exp, 1)
            for g in range(14):
                dst = [bq[:, 0, :], bq[:, 1, :], bq[:, 2, :], bq[:, 3, :], bk[:], bv[:]][g] if g < 6 \
                    else gate[:, g - 6, :]
                evacuate("even_b", g, dst, ACT.Copy if g < 6 else ACT.Silu)
                convert(chunk0["even_b"] + g + 4)
                if g == 7:
                    act.wait_ge(v_turned, 2)
                    act.activation(bv_tok[:], bank[2][:, 0:S].rearrange("p (a b) -> p a b", a=2),
                                   ACT.Copy).then_inc(v_tok, 1)
                    act.wait_ge(g_turned, 1)
                    act.activation(kl_tok[:], bank[5][:].rearrange("p (a b c) -> p a b c", a=2, b=2),
                                   ACT.Copy).then_inc(g_tok, 1)
            for h in range(4):
                act.wait_ge(g_o, 4)
                act.activation(sq[:, h, :], bank[4 + h % 2][:, (h // 2) * S:(h // 2 + 1) * S],
                               ACT.Square).then_inc(g_squared, 1)
            root(rms_gla[:], bank[6][0:H, 0:P], P, g_sums, 1, g_std)
            for h in range(4):
                split(split0["even_o"] + h, act_hi[:, h, :])

            def attention(a, logits_, probs, turned, sinks, splits, hi):
                i = 0
                for u in range(2 * H + 3):
                    if u < 2 * H:
                        w = (u % 2 + 1) * P
                        act.wait_ge(a.negmax, u + 1)
                        if u >= 2:
                            act.wait_ge(a.turned, u - 1)
                        last = act.activation(probs[:, u % 2, 0:w], logits_[:, u % 2, 0:w], ACT.Exp,
                                              bias=small[:, u:u + 1], accum_out=small[:, 16 + u:17 + u])
                        if sinks:
                            s = (u // 2 % 2) * 4 + u // 4
                            last = act.activation(small[:, 32 + u:33 + u], V("sinks", s, 1), ACT.Exp,
                                                  bias=small[:, u:u + 1])
                        last.then_inc(a.probs, 1)
                    if 1 <= u <= 2 * H:
                        v = u - 1
                        act.wait_ge(a.turned, v + 1)
                        if v >= 4:
                            act.wait_ge(a.values, v // 2 - 1)
                        act.activation(turned[:, v % 4, 0:v % 2 + 1, :],
                                       bank[6 + v % 2][:, 0:(v % 2 + 1) * P].rearrange("p (k q) -> p k q", q=P),
                                       ACT.Copy).then_inc(a.turned_read, 1)
                    while i < len(splits) and (u >= splits[i] or u == 2 * H + 2):
                        split(hi[0] + i, act_hi[:, hi[1] + i, :])
                        i += 1

            attention(window, logit, prob, prob_t, True, [8, 12, 16, 18], (split0["even_o"] + 4, 4))
            output_projection("even_out")

            norm(5, "odd_in")
            bias_part(3)
            for g in range(18):
                dst = cq_o[:, g, :] if g < 8 else ck_o[:, g - 8, :] if g < 10 else gate_o[:, g - 10, :]
                evacuate("odd_f", g, dst, ACT.Copy if g < 10 else ACT.Silu)
                convert(chunk0["odd_f"] + g + 4)
            for j in range(2):
                if j == 1:
                    for tt in range(2):
                        evacuate("odd_v", tt, cv_o[:, tt, :], bank_=2 + tt)
                convert(chunk0["odd_v"] + j + 4)
            attention(blocks, logit_o, prob_o, prob_t_o, False, [6, 8, 10, 12, 14, 16, 18, 18],
                      (split0["odd_o"], 0))
            output_projection("odd_out")
            root(std[:, 0:S], bank[4][:, 0:S], 1, sums_ready, 8, std_ready)

        @block.vector
        def _(dve):
            own = [0]

            def then(ins):
                own[0] += 1
                ins.then_inc(dve_own, 1)
                dve.wait_ge(dve_own, own[0])

            def convert(c, it=None):
                if c >= n_chunks:
                    return
                slot = c % RING
                dve.wait_ge(weight_hi, at(c + 1, it, 8))
                dve.tensor_tensor(w_lo[:, slot, :], raw[:, slot, :], w_hi[:, slot, :].bitcast(fp32),
                                  ALU.subtract).then_inc(weight_lo, 1)

            def modulate(a):
                m, k = divmod(a, KT)
                dve.wait_ge(ada_in[a % RING], 16 * ((ADA_FIRST + a) // RING + 1))
                src, dst, c_ = ada_raw[:, a % RING, :], ada_acc[:, m % 2, :], silu_c[:, k, 0:1]
                if k == 0:
                    if m >= 2:
                        dve.wait_ge(ada_cols, m - 1)
                    dve.tensor_scalar(dst, src, c_, None, ALU.mult).then_inc(ada_used, 1)
                else:
                    dve.wait_ge(ada_used, a)
                    dve.scalar_tensor_tensor(dst, src, c_, dst, ALU.mult, ALU.add).then_inc(ada_used, 1)

            def modulate_pair(a, it):
                q = a % 4
                dve.wait_ge(ada_in[q], at(16 * ((ADA_FIRST + a) // RING + 1), it, 16))
                dve.wait_ge(ada_used, at(a - 1, it, 4))
                dst = ada_acc[:, q % 2, :]
                k = it * 2 + (a % 16) // 2
                dve.scalar_tensor_tensor(dst, ada_raw[:, q, :], silu_c[:, ds(k, 1), 0], dst,
                                         ALU.mult, ALU.add).then_inc(ada_used, 1)

            def clear_accumulators(m):
                dve.wait_ge(ada_cols, m)
                then(dve.memset(ada_acc[:], 0.0))

            def modulation(m):
                b = V("ada_b0", (2 + m) * KT, KT) if m < 4 else V("ada_b1", (m - 4) * KT, KT)
                dve.wait_ge(ada_cols, m + 1)
                dve.tensor_tensor(mods[:, m, :], bank[7][:, (m % 2) * KT:(m % 2 + 1) * KT], b,
                                  ALU.add).then_inc(mods_ready, 1)
                dve.wait_ge(mods_ready, m + 1)

            def gain_of(i, scale, g):
                then(dve.scalar_tensor_tensor(gain[:, i, :], scale, 1.0, g, ALU.add, ALU.mult))

            def normed_tile(i, src, g, rs, shift=None):
                if i >= 4:
                    dve.wait_ge(split_lo, i - 3)
                dst = tile_f32[:, i % 4, :]
                ins = dve.scalar_tensor_tensor(dst, src, g, rs, ALU.mult, ALU.mult)
                if shift is not None:
                    then(ins)
                    ins = dve.tensor_scalar(dst, dst, shift, None, ALU.add)
                ins.then_inc(split_src, 1)

            def inverse_root(tok, number):
                dve.wait_ge(std_ready, number)
                then(dve.reciprocal(rstd[:, tok], std[:, tok]))

            def norm(number, name, g, shift=None):
                inverse_root(slice(0, S), number + 2)
                for k in range(KT):
                    normed_tile(split0[name] + k, x[:, k, :], g(k), rstd[:, 0:S],
                                None if shift is None else shift(k))

            def residual(name, g, gate=None, it=None, groups=0, steps=0):
                n = group0[name] + g
                dve.wait_ge(matmul_steps, at(after_group[n], it, steps))
                dve.wait_ge(evacuated, at(n, it, groups))
                if it is None:
                    dst, src = x[:, g, :], bank[n % 2][:, 0:S]
                else:
                    dst, src = x[:, ds(it * groups + g, 1), :], bank[n % 2][:, 0:S].unsqueeze(1)
                if gate is None:
                    dve.tensor_tensor(dst, src, dst, ALU.add).then_inc(evacuated, 1)
                else:
                    dve.scalar_tensor_tensor(dst, src, gate, dst, ALU.mult, ALU.add).then_inc(evacuated, 1)

            dve.wait_ge(small_in, 32)
            for m in range(2):
                dve.wait_ge(first_used, (m + 1) * KT)
                for half in range(2):
                    ins = dve.tensor_copy(mod_rows[:, m * D + half * 512:m * D + (half + 1) * 512],
                                          bank[2 * m + half][0:2, :])
                ins.then_inc(rows_ready, 1)
            inverse_root(slice(CTX, SC), 1)
            dve.wait_ge(first_cols, 2)
            then(dve.tensor_tensor(mod_in[:], bank[7][:, 0:32].rearrange("p (m c) -> p m c", c=2),
                                   V("ada_b0", 0, 16).unsqueeze(2).to_broadcast([P, 16, 2]), ALU.add))
            for s_ in range(2):
                gain_of(s_, mod_in[:, KT:2 * KT, s_], V("norm_mix_g", 0, KT))
            dve.wait_ge(x_in_sem, 16)
            for k in range(KT):
                normed_tile(k, x[:, k, :], gain[:, 0, k:k + 1], rstd[:, CTX:SC], mod_in[:, k, 0:1])
                if k in (1, 3):
                    convert(k // 2)
            convert(2)
            inverse_root(slice(0, CTX), 2)
            dve.wait_ge(ctx_in_sem, 16)
            for k in range(KT):
                normed_tile(KT + k, ctx[:, k, :], gain[:, 1, k:k + 1], rstd[:, 0:CTX], mod_in[:, k, 1:2])
                if k == 3:
                    convert(3)
            convert(4)
            modulate(0)
            convert(5)
            modulate(1)
            convert(6)
            convert(7)
            dve.wait_ge(lora_std, 1)
            then(dve.reciprocal(rstd[:, CTX:SC], std[:, CTX:SC]))
            for k in range(3):
                normed_tile(split0["cq"] + k, cq[:, k, :], V("q_a_norm", k, 1), rstd[:, CTX:SC])
            modulate(2)
            convert(8)
            modulate(3)
            convert(9)
            dve.wait_ge(lora_std, 2)
            dve.reciprocal(rstd[:], std[:]).then_inc(lora_rstd, 1)
            convert(10)
            dve.wait_ge(lora_rstd, 1)
            for k in range(4):
                tok = slice((k % 2) * S, (k % 2 + 1) * S)
                normed_tile(split0["ckv"] + k, ckv[:, k // 2, tok], V("kv_a_norm", k // 2, 1), rstd[:, tok])
            then(dve.tensor_tensor(gqk[:], V("q_g_nope"), V("k_g_nope"), ALU.mult))
            for c in range(4, 12):
                if c > 6:
                    convert(c + 4)
                modulate(c)
            modulation(0)
            for p_ in range(4):
                dve.wait_ge(q_squared, H + p_ + 1)
                dve.tensor_scalar(qr[:, p_, :], qr[:, p_, :], V("q_g_rope"), None, ALU.mult).then_inc(pe_gained, 1)
            dve.tensor_scalar(kpe[:], kpe[:], V("k_g_rope"), None, ALU.mult).then_inc(pe_gained, 1)
            dve.wait_ge(q_sums_read, 1)
            dve.tensor_tensor(small[:, 32:48].rearrange("p (q h) -> p q h", q=2),
                              small[:, 0:32].rearrange("p (q s h) -> p q s h", q=2, s=2)[:, :, 0, :],
                              small[:, 0:32].rearrange("p (q s h) -> p q s h", q=2, s=2)[:, :, 1, :],
                              ALU.add).then_inc(q_sum_added, 1)
            for c in (12, 13):
                convert(c + 4)
                modulate(c)
            dve.wait_ge(rotated, 5)
            dve.wait_ge(rope_in, 16)
            for p_ in range(5):
                v = qr[:, p_, :] if p_ < 4 else kpe[:, CTX:SC]
                r = bank[4 + p_ // 2][:, (p_ % 2) * S:(p_ % 2 + 1) * S] if p_ < 4 else bank[3][:, 0:S]
                dve.tensor_tensor(p_mla[:, 0, 0:S], r, sin, ALU.mult)
                then(dve.tensor_tensor(v, v, cos, ALU.mult))
                then(dve.tensor_tensor(v, v, p_mla[:, 0, 0:S], ALU.add))
            dve.wait_ge(q_std, 1)
            then(dve.reciprocal(q_scale[:, 1], q_scale[:, 0]))
            then(dve.tensor_scalar(q_scale[:, 0], q_scale[:, 1], QK ** -0.5, None, ALU.mult))
            dve.tensor_scalar(q_scale[:, 1], q_scale[:, 0], -1.0, None, ALU.mult).then_inc(q_ready, 1)
            dve.wait_ge(q_ready, 1)
            dve.wait_ge(k_std, 1)
            dve.reciprocal(rstd[0:H, :], std[0:H, :]).then_inc(k_rstd, 1)
            convert(18)
            modulate(14)
            convert(19)

            def final_key(h):
                r = slice((h % 2) * ROPE, (h % 2 + 1) * ROPE)
                dve.wait_ge(k_spread, h + 1)
                dve.scalar_tensor_tensor(kn[:, h, :], kn[:, h, :], gqk[:], bank[h % 2][:], ALU.mult, ALU.mult)
                dve.tensor_tensor(kr[r, h // 2, :], kpe[r, :], bank[h % 2][r, :], ALU.mult).then_inc(k_ready, 1)

            def normalise(a, u, dst, sinks=False, rows=64):
                dve.wait_ge(a.probs, u + 1)
                total = small[:, rows + u:rows + u + 1]
                if sinks:
                    total = small[:, 64 + u:65 + u]
                    then(dve.tensor_tensor(total, small[:, rows + u:rows + u + 1], small[:, 32 + u:33 + u], ALU.add))
                then(dve.reciprocal(small[:, 80 + u:81 + u], total))
                dve.tensor_scalar(dst, dst, small[:, 80 + u:81 + u], None, ALU.mult).then_inc(a.normed, 1)

            final_key(0)
            final_key(1)
            modulate(15)
            for u in range(2 * H + 4):
                h, qt = divmod(u, 2)
                if u < 2 * H:
                    dve.wait_ge(latent.scores, u + 1)
                    then(dve.reduce_max(small[:, u:u + 1], bank[4 + u % 2][:], AX.X))
                    dve.tensor_tensor(small[:, 48 + u:49 + u], small[:, u:u + 1], q_scale[:, 1, qt, h:h + 1],
                                      ALU.mult).then_inc(latent.negmax, 1)
                if 1 <= u <= 2 * H:
                    normalise(latent, u - 1, p_mla[:, (u - 1) % 2, :])
                if u == 1:
                    modulation(1)
                if u < 2 * H:
                    if qt == 0 and h + 2 < H:
                        final_key(h + 2)
                    if qt == 1:
                        modulate(16 + u - 1)
                        modulate(16 + u)
                if qt == 0 and 2 <= h < H + 2:
                    i = split0["mla_o"] + h - 2
                    dve.wait_ge(latent.values, h - 1)
                    dve.wait_ge(split_lo, i - 3)
                    dve.tensor_copy(tile_f32[:, i % 4, :], bank[2 + h % 2][:, 0:S]).then_inc(split_src, 1)
            modulation(2)
            gain_of(2, mods[:, 2, :], V("norm_ffn_g", 0, KT))
            for g in range(KT):
                residual("mla_out", g, mods[:, 0, g:g + 1])
                convert(chunk0["mla_out"] + g + 4)

            def ffn(stage, pairs, gate):
                up, down_ = stage + "_up", stage + "_down"
                if pairs:
                    clear_accumulators(4)
                with dve.Fori(0, 4) as it:
                    for g in range(8):
                        if pairs and g % 2 == 0:
                            modulate_pair(32 + g // 2, it)
                        convert(chunk0[up] + g + 4, it)
                if pairs:
                    modulation(4)
                    modulation(5)
                    gain_of(3, mods[:, 5, :], V("norm_mix_g", KT, KT))
                    clear_accumulators(6)
                with dve.Fori(0, 4) as it:
                    for j in range(8):
                        if pairs and j % 2 == 0:
                            modulate_pair(48 + j // 2, it)
                        if j % 4 == 3:
                            residual(down_, j // 4, mods[:, gate, ds(it * 2 + j // 4, 1)], it, 2, 8)
                        convert(chunk0[down_] + j + 4, it)

            norm(1, "ffn0_in", lambda k: gain[:, 2, k:k + 1], lambda k: mods[:, 1, k:k + 1])
            modulation(3)
            ffn("ffn0", True, 3)

            norm(2, "gm_in", lambda k: gain[:, 3, k:k + 1], lambda k: mods[:, 4, k:k + 1])
            modulation(6)
            modulation(7)
            clear_accumulators(8)
            with dve.Fori(0, 2) as it:
                for j in range(8):
                    convert(chunk0["gm_v"] + j + 4, it)
                    if j % 2 == 1:
                        modulate_pair(64 + j // 2, it)
                    if j % 4 == 3:
                        b = j // 4
                        for tt in range(2):
                            dve.wait_ge(evacuated, at(group0["gm_v"] + 2 * b + tt + 1, it, 4))
                            if 2 * b + tt > 0:
                                dve.wait_ge(ln_counted, at(2 * b + tt, it, 4))
                            dve.bn_stats(ln_stats[:, tt, ds(it * 2 + b, 1), :],
                                         v_gm[:, tt, ds(it * 1024 + b * 512, 512)]).then_inc(ln_counted, 1)
            dve.wait_ge(ln_counted, 8)
            for tt in range(2):
                dve.bn_aggr(ln_mv[:, tt, 0:2], ln_stats[:, tt, :, :]).then_inc(ln_var, 1)
            for tt in range(2):
                dve.wait_ge(ln_std, tt + 1)
                then(dve.reciprocal(ln_mv[:, tt, 3:4], ln_mv[:, tt, 2:3]))
                dve.tensor_scalar(v_gm[:, tt, :], v_gm[:, tt, :], ln_mv[:, tt, 0:1], ln_mv[:, tt, 3:4],
                                  ALU.subtract, ALU.mult).then_inc(v_normed, 1)
            dve.wait_ge(ws_sum_ready, 2)
            dve.wait_ge(gm_in, 32)
            for t in range(GM // P):
                ins = dve.scalar_tensor_tensor((bs_all if t % 2 else mix_bias)[:, t // 2, :], ws_sum[:, t // 2, :],
                                               V("gm_ln_b", t, 1), bs_all[:, t // 2, :], ALU.mult, ALU.add)
            then(ins)
            with dve.Fori(0, 2) as it:
                for j in range(8):
                    if j % 2 == 0:
                        modulate_pair(72 + j // 2, it)
                    convert(chunk0["gm_u"] + j + 4, it)
            dve.wait_ge(evacuated, group0["gm_out"])
            for t in range(GM // P):
                i = split0["gm_s"] + t
                dst = tile_f32[:, i % 4, :].rearrange("p (n q) -> p n q", n=2)
                dve.wait_ge(mixed, t + 1)
                dve.wait_ge(split_lo, i - 3)
                then(dve.scalar_tensor_tensor(dst, bank[4 + t % 2][:, 0:S].rearrange("p (n q) -> p n q", n=2),
                                              V("gm_ln_g", t, 1),
                                              (bs_all if t % 2 else mix_bias)[:, t // 2:t // 2 + 1, :].to_broadcast([P, 2, P]), ALU.mult, ALU.add))
                dve.tensor_tensor(tile_f32[:, i % 4, :], tile_f32[:, i % 4, :], u_gm[:, t, :],
                                  ALU.mult).then_inc(split_src, 1)
            modulation(8)
            gain_of(4, mods[:, 8, :], V("norm_ffn_g", KT, KT))
            with dve.Fori(0, 2) as it:
                for j in range(8):
                    if j % 2 == 1:
                        residual("gm_out", j // 2, mods[:, 6, ds(it * 4 + j // 2, 1)], it, 4, 8)
                    convert(chunk0["gm_out"] + j + 4, it)

            norm(3, "ffn1_in", lambda k: gain[:, 4, k:k + 1], lambda k: mods[:, 7, k:k + 1])
            modulation(9)
            ffn("ffn1", False, 9)

            norm(4, "even_in", lambda k: V("norm_gain_2", k, 1))
            for j in range(5):
                convert(chunk0["even_a"] + j + 4)
            dve.wait_ge(g_z, 2)
            for t in range(2):
                dve.tensor_scalar(z[:, t, :], bank[4][:, t * S:(t + 1) * S], V("gla_b_up", t, 1), None,
                                  ALU.add).then_inc(g_z_ready, 1)
            dve.wait_ge(g_ln, 1)
            then(dve.scalar_tensor_tensor(z[:], z[:], 0.0, zl[:], ALU.min, ALU.subtract))
            then(dve.tensor_tensor_scan(cum[:].rearrange("p a b -> p (a b)"), masks[:, 0:2 * S],
                                        z[:].rearrange("p a b -> p (a b)"), 0.0, ALU.mult, ALU.add))
            dve.tensor_scalar(decay[:, 0], cum[:].rearrange("p a (n c) -> p a n c", n=4)[:, :, :, 63],
                              1.0 / TAU, None, ALU.mult).then_inc(g_last, 1)
            for j in range(4):
                convert(chunk0["even_av"] + j + 4)
            dve.wait_ge(g_exp, 1)
            dve.scalar_tensor_tensor(qe[:], aq[:], 0.125, e_pos[:], ALU.mult, ALU.mult)
            dve.tensor_tensor(ke[:], ak[:], e_neg[:], ALU.mult)
            dve.tensor_tensor(kl[:], ak[:], e_last[:], ALU.mult).then_inc(g_factors, 1)
            for j in range(14):
                convert(chunk0["even_b"] + j + 4)
            dve.wait_ge(att_zero, 1)
            dve.wait_ge(g_att, 8)
            causal = masks[:, 2 * S:2 * S + P].bitcast(mybir.dt.uint32)
            for tt in range(2):
                dve.copy_predicated(att[:, 4 * tt:4 * tt + 4, :],
                                    causal.unsqueeze(1).to_broadcast([P, 4, P]),
                                    bank[2 + tt][:].rearrange("p (h c) -> p h c", h=4)).then_inc(g_att_ready, 1)
            dve.wait_ge(g_kv, 3)
            for n in range(3):
                kv = bank[6 + n % 2][:, (n // 2) * S:(n // 2 + 1) * S].rearrange("p (t d) -> p t d", t=2)
                if n == 0:
                    dve.tensor_copy(state[:, 0, :, :], kv).then_inc(g_state, 1)
                else:
                    dve.wait_ge(g_state, n)
                    dve.scalar_tensor_tensor(state[:, n, 0, :], state[:, n - 1, 0, :], decay[:, 1, 0, n:n + 1],
                                             kv[:, 0, :], ALU.mult, ALU.add)
                    dve.scalar_tensor_tensor(state[:, n, 1, :], state[:, n - 1, 1, :], decay[:, 1, 1, n:n + 1],
                                             kv[:, 1, :], ALU.mult, ALU.add).then_inc(g_state, 1)
            dve.wait_ge(g_std, 1)
            dve.reciprocal(rms_gla[:], rms_gla[:]).then_inc(g_rstd, 1)
            for h in range(4):
                i = split0["even_o"] + h
                dve.wait_ge(split_lo, i - 3)
                dve.wait_ge(g_spread, 4 * (h // 2) + 4)
                then(dve.scalar_tensor_tensor(o_gla[:, h % 2, :], gate[:, h, :], V("gla_gain"),
                                              bank[6 + h // 2][:, (h % 2) * S:(h % 2 + 1) * S],
                                              ALU.mult, ALU.mult))
                dve.tensor_tensor(tile_f32[:, i % 4, :], bank[4 + h % 2][:, (h // 2) * S:(h // 2 + 1) * S],
                                  o_gla[:, h % 2, :], ALU.mult).then_inc(split_src, 1)

            def attention(a, logits_, probs, sinks, scale, bias_of, value_tile, i0, gates):
                for u in range(2 * H + 4):
                    h, qt = divmod(u, 2)
                    w = (qt + 1) * P
                    if u < 2 * H:
                        dve.wait_ge(a.scores, u + 1)
                        if u >= 2:
                            dve.wait_ge(a.probs, u - 1)
                        dve.scalar_tensor_tensor(logits_[:, u % 2, 0:w], bank[4 + u % 2][:, 0:w], scale,
                                                 bias[:, bias_of(h), S - w:S], ALU.mult,
                                                 ALU.add).then_inc(a.logits, 1)
                        dve.wait_ge(a.logits, u + 1)
                        then(dve.reduce_max(small[:, 48 + u:49 + u], logits_[:, u % 2, 0:w], AX.X))
                        if sinks:
                            dve.tensor_scalar(small[:, u:u + 1], small[:, 48 + u:49 + u],
                                              V("sinks", bias_of(h), 1), -1.0, ALU.max,
                                              ALU.mult).then_inc(a.negmax, 1)
                        else:
                            dve.tensor_scalar(small[:, u:u + 1], small[:, 48 + u:49 + u], -1.0, None,
                                              ALU.mult).then_inc(a.negmax, 1)
                    if 1 <= u <= 2 * H:
                        v = u - 1
                        normalise(a, v, probs[:, v % 2, 0:(v % 2 + 1) * P], sinks, 16)
                    slot = value_tile(u)
                    if slot is not None:
                        heads_done = (slot + 1) * (2 if sinks else 1)
                        dve.wait_ge(a.values, heads_done)
                        dve.wait_ge(split_lo, i0 + slot - 3)
                        dve.tensor_tensor(tile_f32[:, (i0 + slot) % 4, :], bank[2 + slot % 2][:, 0:S],
                                          gates[:, slot, :], ALU.mult).then_inc(split_src, 1)

            attention(window, logit, prob, True, 0.125, lambda h: (h % 2) * 4 + h // 2,
                      lambda u: (u - 7) // 4 if u >= 7 and u % 4 == 3 else None,
                      split0["even_o"] + 4, gate[:, 4:8, :])
            for g in range(KT):
                residual("even_out", g)
                convert(chunk0["even_out"] + g + 4)

            norm(5, "odd_in", lambda k: V("norm_gain_2", KT + k, 1))
            for j in range(18 + 2):
                convert(chunk0["odd_f"] + j + 4)
            attention(blocks, logit_o, prob_o, False, P ** -0.5, lambda h: H + h,
                      lambda u: (u - 5) // 2 if u >= 5 and u % 2 == 1 else None, split0["odd_o"], gate_o)
            for g in range(KT):
                residual("odd_out", g)
                convert(chunk0["odd_out"] + g + 4)
            inverse_root(slice(0, S), 8)
            for k in range(KT):
                dve.scalar_tensor_tensor(result[:, k, :], x[:, k, :], V("final_gain", k, 1), rstd[:, 0:S],
                                         ALU.mult, ALU.mult).then_inc(out_ready, 1)

        @block.gpsimd
        def _(pool):
            def split(i, hi, lo):
                pool.wait_ge(split_hi, i + 1)
                pool.tensor_tensor(lo, tile_f32[:, i % 4, :], hi.bitcast(fp32), ALU.subtract).then_inc(split_lo, 1)

            def sum_squares(norm):
                for k in range(1, KT - 1):
                    pool.wait_ge(squared, squares_before(norm) + k + 1)
                    if k > 1:
                        pool.wait_ge(square_sums, norm * (KT - 2) + k - 1)
                    pool.tensor_tensor(square_sum[:], sq[:, 0, :] if k == 1 else square_sum[:], sq[:, k, :],
                                       ALU.add).then_inc(square_sums, 1)

            def split_input(name):
                for k in range(KT):
                    split(split0[name] + k, act_hi[:, k, :], act_lo[:, k, :])

            pool.memset(ones[:], 1.0).then_inc(setup, 1)
            pool.memset(eps[:], EPS).then_inc(setup, 1)
            pool.memset(mean[:], 1.0 / D).then_inc(setup, 1)
            sum_squares(0)
            for k in range(KT):
                split(k, in_hi[:, k, CTX:SC], in_lo[:, k, CTX:SC])
            for k in range(KT):
                split(KT + k, in_hi[:, k, 0:CTX], in_lo[:, k, 0:CTX])
            for k in range(3):
                split(split0["cq"] + k, cq_hi[:, k, :], cq_lo[:, k, :])
            for i in range(12):
                pool.wait_ge(evacuated, group0["q_b"] + i + 1)
                if i >= 8:
                    pool.wait_ge(q_sums, i - 7)
                q = qn[:, i, :] if i < H else qr[:, i - H, :]
                pool.tensor_tensor(sq[:, i % 8, :], q, q, ALU.mult).then_inc(q_squared, 1)
                if i == 3:
                    for k in range(4):
                        tok = slice((k % 2) * S, (k % 2 + 1) * S)
                        split(split0["ckv"] + k, ckv_hi[:, k // 2, tok], ckv_lo[:, k // 2, tok])
            pool.wait_ge(q_sums, 12)
            for h in range(H):
                pool.wait_ge(evacuated, group0["kv_b_k"] + h + 1)
                if h >= 4:
                    pool.wait_ge(k_sums, h - 3)
                pool.tensor_tensor(sq_k(h), kn[:, h, :], kn[:, h, :], ALU.mult).then_inc(k_squared, 1)
            split_input("mla_o")
            sum_squares(1)

            def ffn(stage, norm):
                split_input(stage + "_in")
                with pool.Fori(0, 4) as it:
                    for g in range(8):
                        i = split0[stage + "_hid"] + g
                        pool.wait_ge(evacuated, at(group0[stage + "_up"] + g + 1, it, 8))
                        pool.tensor_tensor(tile_f32[:, i % 4, :], relu[:, g % 2, :], relu[:, g % 2, :],
                                           ALU.mult).then_inc(hid_squared, 1)
                        pool.wait_ge(hid_squared, at(32 * (stage == "ffn1") + g + 1, it, 8))
                        pool.wait_ge(split_hi, at(i + 1, it, 8))
                        pool.tensor_tensor(hid_lo[:, ds(it * 8 + g, 1), :], tile_f32[:, i % 4:i % 4 + 1, :],
                                           hid_hi[:, ds(it * 8 + g, 1), :].bitcast(fp32),
                                           ALU.subtract).then_inc(split_lo, 1)

                sum_squares(norm)

            ffn("ffn0", 2)
            split_input("gm_in")
            pool.dma_start(ws[:], gm_ws).then_inc(gm_in, 16)
            pool.dma_start(sq[:, 4:8, :].rearrange("p a b -> p (a b)"), gm_rows.partition_broadcast(P)).then_inc(gm_in, 16)
            for t in range(GM // P):
                split(split0["gm_s"] + t, s_hi[:, t, :], s_lo[:, t, :])
            sum_squares(3)
            ffn("ffn1", 4)
            split_input("even_in")
            pool.wait_ge(sums_ready, 6)
            pool.dma_start(w_up[:], gla_w_up).then_inc(masks_in, 16)
            pool.dma_start(masks[:], consts["masks"]).then_inc(masks_in, 16)
            pool.memset(att[:], 0.0).then_inc(att_zero, 1)
            split_input("even_o")
            sum_squares(5)
            split_input("odd_in")
            split_input("odd_o")
            sum_squares(6)


def constants():
    const = np.zeros((P, P + 18), np.float32)
    const[:, 0:P] = np.eye(P)
    const[:, P + 7] = 1.0
    const[:ROPE, P + 16], const[ROPE:, P + 17] = 1.0, 1.0
    half = ROPE // 2
    inv = (np.float32(10000.0) ** (-np.arange(0, half, 2, dtype=np.float32) / np.float32(half))).astype(np.float32)
    tok = np.arange(S)
    row, col = (tok // 64).astype(np.float32), (tok % 64).astype(np.float32)
    ang_r, ang_c = row[:, None] * inv[None], col[:, None] * inv[None]
    ang = np.concatenate([ang_r, ang_r, ang_c, ang_c], -1).astype(np.float32)
    rotation = np.zeros((ROPE, ROPE), np.float32)
    q = ROPE // 4
    for a in range(q):
        rotation[a, q + a], rotation[q + a, a] = -1, 1
        rotation[2 * q + a, 3 * q + a], rotation[3 * q + a, 2 * q + a] = -1, 1
    rope = np.zeros((P, P + 2 * S), np.float32)
    for r in range(2):
        f = slice(r * ROPE, (r + 1) * ROPE)
        rope[f, f] = rotation.T
        rope[f, P:P + S], rope[f, P + S:] = np.cos(ang).T, np.sin(ang).T
    dist = 255 - np.arange(MASKW)
    n = np.maximum(dist, 0)
    nf = np.maximum(n, 1).astype(np.float32)
    large = 16 + (np.log(nf / np.float32(16)) / np.float32(np.log(8.0)) * np.float32(16)).astype(np.int32)
    bucket = np.where(n < 16, n, np.minimum(large, 31))
    onehot = np.zeros((33, 2, MASKW), np.float32)
    onehot[bucket, :, np.arange(MASKW)] = 1.0
    onehot[32, 0] = np.where((dist >= 0) & (dist < P), 0.0, NEG)
    onehot[32, 1] = np.where(dist >= 0, 0.0, NEG)
    masks = np.zeros((P, 2 * S + P), np.float32)
    masks[:, 0:2 * S] = np.arange(2 * S) % 64 != 0
    s_, c_ = np.arange(P)[:, None], np.arange(P)[None]
    masks[:, 2 * S:] = (s_ // 64 == c_ // 64) & (s_ <= c_)
    return {"const": const, "rope": rope, "onehot": onehot, "anti": np.eye(P, dtype=np.float32)[::-1].copy(),
            "masks": masks}


def tiles(w, n_out=None):
    k, n = w.shape[0] // P, w.shape[1] // P
    return w.reshape(k, P, n, P).transpose(2, 1, 0, 3)


def chunks_of(w):
    t = tiles(w)
    n, p, k, _ = t.shape
    flat = t.transpose(0, 2, 1, 3).reshape(n * k, P, P)
    per = 6 if k == 3 else 8
    flat = flat.reshape(n * k // per, per, P, P).transpose(0, 2, 1, 3).reshape(-1, P, per * P)
    return np.concatenate([flat, np.zeros((flat.shape[0], P, CW - per * P), w.dtype)], -1)


def chunks_by_token(w, width):
    k, per, n = w.shape[0] // P, CW // width, w.shape[1] // width
    return w.reshape(k // per, per, P, n, width).transpose(3, 0, 2, 1, 4).reshape(-1, P, CW)


def kernel(**inputs):
    import concourse.bacc as bacc
    from concourse.bass_utils import run_bass_kernel_spmd

    a = {k: np.asarray(v) for k, v in inputs.items()}

    def cols(v):
        return v.reshape(-1, P).T

    def feature_major(m):
        return m.T.reshape(-1, P, m.shape[0]).transpose(1, 0, 2)

    both = lambda v: np.concatenate([v, v])
    q_g, k_g = a["mla_q_norm"][0], a["mla_k_norm"][0]
    vecs = {
        "c": cols(a["c"][0]), "c_ctx": cols(a["c_ctx"]), "ada_b0": cols(a["ada_b"][0]),
        "ada_b1": cols(a["ada_b"][1]), "norm_mix_g": cols(a["norm_mix_g"].reshape(-1)),
        "norm_ffn_g": cols(a["norm_ffn_g"].reshape(-1)), "q_a_norm": cols(a["mla_q_a_norm"][0]),
        "kv_a_norm": cols(a["mla_kv_a_norm"][0]), "q_g_nope": cols(q_g[:P]), "q_g_rope": cols(both(q_g[P:])),
        "k_g_nope": cols(k_g[:P]), "k_g_rope": cols(both(k_g[P:])), "gm_ln_g": cols(a["gm_ln_g"][0]),
        "gm_ln_b": cols(a["gm_ln_b"][0]), "norm_gain_2": cols(a["norm_gain_2"].reshape(-1)),
        "final_gain": cols(a["final_gain_2"]), "gla_b_up": cols(a["gla_b_up_2"][0]),
        "gla_gain": cols(a["gla_norm_gain_2"][0]),
        "sinks": np.broadcast_to(a["swa_sinks_2"][0][None], (P, H)),
    }
    vecs = np.ascontiguousarray(np.concatenate([vecs[name] for name, _ in VECS], 1))

    wq_b = a["mla_wq_b"][0].reshape(Q_LORA, H, QK)
    wq_b = np.concatenate([wq_b[:, :, :P].reshape(Q_LORA, -1), wq_b[:, :, P:].reshape(Q_LORA, -1)], 1)
    wkv_a = a["mla_wkv_a"][0]
    wkv_a = np.concatenate([wkv_a, wkv_a[:, KV_LORA:]], 1)
    wkv_b = a["mla_wkv_b"][0].reshape(KV_LORA, H, 2, P)
    w_e, w_o = a["w_in_even_2"][0], a["w_in_odd_2"][0]
    aq, ak, av, down, a_gate, bq, bk, bv, b_gate = np.split(
        w_e, np.cumsum([256, 256, 512, 16, 512, 512, 128, 128]), 1)

    def paired(w):
        return w.reshape(-1, 2, 4, 64).transpose(0, 2, 1, 3).reshape(-1, 512)

    w_out_e = a["w_out_even_2"][0]
    w_out_e = np.concatenate([w_out_e[:512], paired(w_out_e[512:].T).T], 0)
    down = np.concatenate([down, np.zeros((D, P - 16), down.dtype)], 1)
    cq, ck, cv, c_gate = np.split(w_o, np.cumsum([1024, 256, 256]), 1)
    gm_in = a["gm_w_in"][0]
    weights = np.concatenate([
        chunks_of(a["mla_wq_a"][0]), chunks_of(wkv_a), chunks_of(wq_b),
        chunks_of(np.ascontiguousarray(wkv_b[:, :, 0]).reshape(KV_LORA, -1)),
        chunks_by_token(np.ascontiguousarray(wkv_b[:, :, 1]).reshape(KV_LORA, -1), 512),
        chunks_of(a["mla_wo"][0]),
        chunks_of(a["ffn_w1"][0]), chunks_of(a["ffn_w2"][0]),
        chunks_by_token(gm_in[:, GM:], 512), chunks_of(gm_in[:, :GM]), chunks_of(a["gm_w_out"][0]),
        chunks_of(a["ffn_w1"][1]), chunks_of(a["ffn_w2"][1]),
        chunks_of(np.concatenate([down, aq, ak], 1)), chunks_by_token(av, 512),
        chunks_of(np.concatenate([paired(bq), bk, bv, a_gate, paired(b_gate)], 1)), chunks_of(w_out_e),
        chunks_of(np.concatenate([cq, ck, c_gate], 1)), chunks_by_token(cv, 256),
        chunks_of(a["w_out_odd_2"][0]),
    ])
    assert weights.shape == (Count().chunks, P, CW), weights.shape

    ada = a["ada_w"].reshape(2, KT, P, 6, CW)
    ada_chunks = [ada[0, k, :, m] for m in range(6) for k in range(KT)]
    for pair in (0, 2, 4):
        ada_chunks += [ada[1, k, :, pair + m] for k in range(KT) for m in range(2)]
    arrays = {
        "vecs": vecs, "gm_rows": np.ascontiguousarray(a["gm_bs"][0].reshape(-1)),
        "rel_ext": np.concatenate([a["rel_bias_2"], np.ones((1, H), np.float32)], 0),
        "x_in": np.ascontiguousarray(feature_major(a["x"][0])),
        "ctx_in": np.ascontiguousarray(feature_major(a["ctx"][0])),
        "ada": np.stack(ada_chunks), "weights": weights,
        "gm_ws": np.ascontiguousarray(a["gm_ws"][0].transpose(2, 0, 1)),
        "gla_w_up": np.ascontiguousarray(a["gla_w_up_2"][0]),
    }
    consts = constants()
    nc = bacc.Bacc("TRN2", target_bir_lowering=False, num_devices=1)

    def declare(name, v):
        return nc.dram_tensor(name, v.shape, mybir.dt.from_np(v.dtype), kind="ExternalInput").ap()

    args = {name: declare(name, v) for name, v in arrays.items()}
    const_args = {name: declare("const_" + name, v) for name, v in consts.items()}
    out = nc.dram_tensor("out", (P, KT, S), mybir.dt.float32, kind="ExternalOutput").ap()
    build_program(nc, consts=const_args, out=out, **args)
    given = {**arrays, **{"const_" + name: v for name, v in consts.items()}}
    r = run_bass_kernel_spmd(nc, [given], core_ids=[0])
    got = np.asarray(r.results[0]["out"])
    return np.ascontiguousarray(got.transpose(2, 1, 0).reshape(1, S, D))
```
